# Optimizing a Trainium2 kernel written in Bass

```python
import jax, jax.numpy as jnp
from jax import lax
import numpy as np

D_MODEL = 1024
BATCH = 1
SEQ = 256
DEPTH = 2

HEAD_DIM = 64
A_Q_HEADS = 16
A_KV_HEADS = 4
B_GROUPS = ((128, 1), (512, 4), (2048, 16))
N_B_GROUPS = 3
B_HEADS_PER_GROUP = 4
B_HEADS = N_B_GROUPS * B_HEADS_PER_GROUP
GRID_W = 64
ROPE_THETA = 10000.0
ROPE_AXIS_DIM = HEAD_DIM // 2
Q_BLOCK = 128
FFN_HIDDEN = -(-8 * D_MODEL // (3 * 256)) * 256
PLE_DIM = 256
LN_EPS = 1e-5
RMS_EPS = 1e-6
NEG_INF = -1e30
ALPHA = (2 * DEPTH) ** 0.25

A_Q_DIM = A_Q_HEADS * HEAD_DIM
A_KV_DIM = A_KV_HEADS * HEAD_DIM
B_DIM = B_HEADS * HEAD_DIM
B_OUT_DIM = B_HEADS_PER_GROUP * HEAD_DIM
IN_PROJ_DIM = A_Q_DIM + 2 * A_KV_DIM + 3 * B_DIM + 2 * D_MODEL
IN_SPLITS = (A_Q_DIM, A_Q_DIM + A_KV_DIM, A_Q_DIM + 2 * A_KV_DIM,
             A_Q_DIM + 2 * A_KV_DIM + B_DIM, A_Q_DIM + 2 * A_KV_DIM + 2 * B_DIM,
             A_Q_DIM + 2 * A_KV_DIM + 3 * B_DIM)

kernel_name = 'hybrid_axial_gqa_dilated_deepnorm_encoder'

def layer_norm(x, g, b):
    xf = x.astype(jnp.float32)
    mu = jnp.mean(xf, axis=-1, keepdims=True)
    var = jnp.mean(jnp.square(xf - mu), axis=-1, keepdims=True)
    return ((xf - mu) * lax.rsqrt(var + LN_EPS) * g + b).astype(x.dtype)

def rms_norm_heads(x, g):
    xf = x.astype(jnp.float32)
    y = xf * lax.rsqrt(jnp.mean(jnp.square(xf), axis=-1, keepdims=True) + RMS_EPS) * g
    return y.astype(x.dtype)

def axial_rope_tables(seq_len):
    rows = seq_len // GRID_W
    row = jnp.repeat(jnp.arange(rows, dtype=jnp.float32), GRID_W)
    col = jnp.tile(jnp.arange(GRID_W, dtype=jnp.float32), rows)
    inv = ROPE_THETA ** (-jnp.arange(0, ROPE_AXIS_DIM, 2, dtype=jnp.float32) / ROPE_AXIS_DIM)
    ang = jnp.concatenate([row[:, None] * inv, col[:, None] * inv], axis=-1)
    return jnp.cos(ang), jnp.sin(ang)

def rope_axis(xa, c, s):
    half = xa.shape[-1] // 2
    x1, x2 = xa[..., :half], xa[..., half:]
    c = c[None, :, None, :]
    s = s[None, :, None, :]
    return jnp.concatenate([x1 * c - x2 * s, x2 * c + x1 * s], axis=-1)

def apply_axial_rope(x, cos, sin):
    h = ROPE_AXIS_DIM // 2
    xr = rope_axis(x[..., :ROPE_AXIS_DIM], cos[:, :h], sin[:, :h])
    xc = rope_axis(x[..., ROPE_AXIS_DIM:], cos[:, h:], sin[:, h:])
    return jnp.concatenate([xr, xc], axis=-1).astype(x.dtype)

def axial_gqa(q, k, v):
    bsz, seq = q.shape[0], q.shape[1]
    grp = A_Q_HEADS // A_KV_HEADS
    nb = seq // Q_BLOCK
    qb = q.reshape(bsz, nb, Q_BLOCK, A_KV_HEADS, grp, HEAD_DIM).transpose(1, 0, 2, 3, 4, 5)
    scale = HEAD_DIM ** -0.5

    def one_block(qblk):
        s = jnp.einsum('bqkgd,bskd->bkgqs', qblk, k).astype(jnp.float32) * scale
        p = jax.nn.softmax(s, axis=-1)
        return jnp.einsum('bkgqs,bskd->bqkgd', p.astype(v.dtype), v)

    o = lax.map(one_block, qb)
    return o.transpose(1, 0, 2, 3, 4, 5).reshape(bsz, seq, A_Q_DIM)

def alibi_slopes(n):
    return 2.0 ** (-8.0 * jnp.arange(1, n + 1, dtype=jnp.float32) / n)

def dilated_group(q, k, v, window, dilation, slopes):
    bsz, seq, nh, _ = q.shape
    nb = seq // Q_BLOCK
    n_side = (window // 2) // dilation
    offs = dilation * jnp.arange(-n_side, n_side + 1, dtype=jnp.int32)
    bias = -slopes[:, None, None] * jnp.abs(offs).astype(jnp.float32)[None, None, :]
    scale = HEAD_DIM ** -0.5

    def one_block(bi):
        start = bi * Q_BLOCK
        t = start + jnp.arange(Q_BLOCK, dtype=jnp.int32)
        idx = t[:, None] + offs[None, :]
        valid = (idx >= 0) & (idx < seq)
        idx = jnp.clip(idx, 0, seq - 1)
        qblk = lax.dynamic_slice_in_dim(q, start, Q_BLOCK, axis=1)
        kg = jnp.take(k, idx, axis=1)
        vg = jnp.take(v, idx, axis=1)
        s = jnp.einsum('bqhd,bqjhd->bhqj', qblk, kg).astype(jnp.float32) * scale + bias
        s = jnp.where(valid[None, None], s, NEG_INF)
        lse = jax.nn.logsumexp(s, axis=-1)
        p = jnp.exp(s - lse[..., None])
        o = jnp.einsum('bhqj,bqjhd->bqhd', p.astype(v.dtype), vg)
        return o, lse

    o, lse = lax.map(one_block, jnp.arange(nb, dtype=jnp.int32))
    o = o.transpose(1, 0, 2, 3, 4).reshape(bsz, seq, nh, HEAD_DIM)
    lse = lse.transpose(1, 0, 3, 2).reshape(bsz, seq, nh)
    return o, lse

def dilated_mixture(q, k, v):
    bsz, seq = q.shape[0], q.shape[1]
    slopes = alibi_slopes(B_HEADS).reshape(N_B_GROUPS, B_HEADS_PER_GROUP)
    outs, lses = [], []
    for g, (window, dilation) in enumerate(B_GROUPS):
        o, l = dilated_group(q[:, :, g], k[:, :, g], v[:, :, g], window, dilation, slopes[g])
        outs.append(o)
        lses.append(l)
    wts = jax.nn.softmax(jnp.stack(lses, axis=0), axis=0)
    o = jnp.sum(wts[..., None].astype(outs[0].dtype) * jnp.stack(outs, axis=0), axis=0)
    return o.reshape(bsz, seq, B_OUT_DIM)

def hybrid_layer(x, p_i, w_in, b_gate, q_norm_g, k_norm_g, w_branch_a, w_branch_b, w_out,
                 ln1_g, ln1_b, w_ffn_in, w_ffn_out, ln2_g, ln2_b, w_ple_proj, w_ple_gate,
                 cos, sin):
    bsz, seq, _ = x.shape
    proj = x @ w_in
    qa, ka, va, qb, kb, vb, gates = jnp.split(proj, IN_SPLITS, axis=-1)
    qa = apply_axial_rope(rms_norm_heads(qa.reshape(bsz, seq, A_Q_HEADS, HEAD_DIM), q_norm_g), cos, sin)
    ka = apply_axial_rope(rms_norm_heads(ka.reshape(bsz, seq, A_KV_HEADS, HEAD_DIM), k_norm_g), cos, sin)
    va = va.reshape(bsz, seq, A_KV_HEADS, HEAD_DIM)
    o_a = axial_gqa(qa, ka, va)
    bshape = (bsz, seq, N_B_GROUPS, B_HEADS_PER_GROUP, HEAD_DIM)
    o_b = dilated_mixture(qb.reshape(bshape), kb.reshape(bshape), vb.reshape(bshape))
    g_a, g_b = jnp.split(jax.nn.sigmoid(gates + b_gate), 2, axis=-1)
    u = g_a * (o_a @ w_branch_a) + g_b * (o_b @ w_branch_b)
    x = layer_norm(ALPHA * x + u @ w_out, ln1_g, ln1_b)
    hg, hu = jnp.split(x @ w_ffn_in, 2, axis=-1)
    f = (jax.nn.silu(hg) * hu) @ w_ffn_out
    pe = jax.nn.sigmoid(x @ w_ple_gate) * (p_i @ w_ple_proj)
    return layer_norm(ALPHA * x + f + pe, ln2_g, ln2_b)

def setup_inputs(seed: int = 0) -> dict:
    key = jax.random.key(seed)
    ks = jax.random.split(key, 24)
    beta = (8 * DEPTH) ** -0.25
    f32 = jnp.float32

    def nrm(k, shape, scale):
        return jax.random.normal(k, shape, f32) * scale

    def gain(k, shape):
        return 1.0 + 0.02 * jax.random.normal(k, shape, f32)

    return {
        'x': jax.random.normal(ks[0], (BATCH, SEQ, D_MODEL), f32),
        'p': jax.random.normal(ks[1], (DEPTH, BATCH, SEQ, PLE_DIM), f32),
        'ln_emb_g': gain(ks[2], (D_MODEL,)),
        'ln_emb_b': nrm(ks[3], (D_MODEL,), 0.02),
        'w_in': nrm(ks[4], (DEPTH, D_MODEL, IN_PROJ_DIM), D_MODEL ** -0.5),
        'b_gate': nrm(ks[5], (DEPTH, 2 * D_MODEL), 0.02),
        'q_norm_g': gain(ks[6], (DEPTH, HEAD_DIM)),
        'k_norm_g': gain(ks[7], (DEPTH, HEAD_DIM)),
        'w_branch_a': nrm(ks[8], (DEPTH, A_Q_DIM, D_MODEL), A_Q_DIM ** -0.5),
        'w_branch_b': nrm(ks[9], (DEPTH, B_OUT_DIM, D_MODEL), B_OUT_DIM ** -0.5),
        'w_out': nrm(ks[10], (DEPTH, D_MODEL, D_MODEL), beta * D_MODEL ** -0.5),
        'ln1_g': gain(ks[11], (DEPTH, D_MODEL)),
        'ln1_b': nrm(ks[12], (DEPTH, D_MODEL), 0.02),
        'w_ffn_in': nrm(ks[13], (DEPTH, D_MODEL, 2 * FFN_HIDDEN), D_MODEL ** -0.5),
        'w_ffn_out': nrm(ks[14], (DEPTH, FFN_HIDDEN, D_MODEL), beta * FFN_HIDDEN ** -0.5),
        'ln2_g': gain(ks[15], (DEPTH, D_MODEL)),
        'ln2_b': nrm(ks[16], (DEPTH, D_MODEL), 0.02),
        'w_ple_proj': nrm(ks[17], (DEPTH, PLE_DIM, D_MODEL), PLE_DIM ** -0.5),
        'w_ple_gate': nrm(ks[18], (DEPTH, D_MODEL, D_MODEL), D_MODEL ** -0.5),
    }

def reference(x, p, ln_emb_g, ln_emb_b, w_in, b_gate, q_norm_g, k_norm_g, w_branch_a,
              w_branch_b, w_out, ln1_g, ln1_b, w_ffn_in, w_ffn_out, ln2_g, ln2_b,
              w_ple_proj, w_ple_gate):
    seq = x.shape[1]
    cos, sin = axial_rope_tables(seq)
    x = layer_norm(x, ln_emb_g, ln_emb_b)
    for i in range(DEPTH):
        x = hybrid_layer(x, p[i], w_in[i], b_gate[i], q_norm_g[i], k_norm_g[i],
                         w_branch_a[i], w_branch_b[i], w_out[i], ln1_g[i], ln1_b[i],
                         w_ffn_in[i], w_ffn_out[i], ln2_g[i], ln2_b[i],
                         w_ple_proj[i], w_ple_gate[i], cos, sin)
    return x


_drawn_inputs = setup_inputs


def setup_inputs(seed=0):
    import zlib

    import numpy as np

    out = dict(_drawn_inputs(seed))
    spreads = {}
    factors = {'ln_emb_g': 2.96, 'ln_emb_b': 3.05, 'b_gate': 8.0, 'q_norm_g': 8.0, 'k_norm_g': 8.0}
    for name, (base, spread) in spreads.items():
        noise = np.random.default_rng([zlib.crc32(name.encode()), seed]).standard_normal(out[name].shape)
        drawn = base * np.exp(spread * noise) if base else spread * noise
        out[name] = __import__('jax').numpy.asarray(drawn.astype(out[name].dtype))
    for name, factor in factors.items():
        out[name] = (out[name] * factor).astype(out[name].dtype)
    return out
```

```python
import concourse.bass as bass
from concourse import mybir
from contextlib import ExitStack

F32 = mybir.dt.float32
F32R = mybir.dt.float32r
ALU = mybir.AluOpType
ACT = mybir.ActivationFunctionType
AX_X = mybir.AxisListType.X

P = 128
D = 1024
SEQ = 256
TILES = SEQ // P
KT = D // P
DEPTH = 2
HEAD = 64
A_HEADS, A_KV = 16, 4
B_GROUPS, B_PER_GROUP = 3, 4
A_Q, A_KVD, B_D = A_HEADS * HEAD, A_KV * HEAD, B_GROUPS * B_PER_GROUP * HEAD
FFN = -(-8 * D // (3 * 256)) * 256
PLE = 256
ALPHA = (2 * DEPTH) ** 0.25
LN_EPS, RMS_EPS = 1e-5, 1e-6
SCALE = HEAD ** -0.5
QA0, KA0 = 0, A_Q
QB0 = A_Q + 2 * A_KVD
KB0, VB0 = QB0 + B_D, QB0 + 2 * B_D
GATE0 = QB0 + 3 * B_D
N_B_HEADS = B_GROUPS * B_PER_GROUP
SLOPE = [2.0 ** (-8.0 * (n + 1) / N_B_HEADS) for n in range(N_B_HEADS)]

WORDS = 2048
RING = 3
C_KB, C_QB, C_VB = 0, 3, 6
C_KV, C_QA = 9, 11
C_GB, C_GA = 15, 19
C_BB, C_BA = 23, 25
C_WO, C_PP, C_PG = 29, 33, 35
POOL_STEPS, TABLES = 15, 14
C_FF = 39
FB = FFN // 256
CHUNKS = C_FF + 3 * FB
assert CHUNKS == 72 and CHUNKS % RING == 0 and C_FF % RING == 0 and FB % 2 == 1
AHEAD = 2

GAP_CHUNK = 7
B_ITEMS = B_PER_GROUP * TILES
A_ITEMS = A_HEADS
ITEMS = B_ITEMS + A_ITEMS
A_GAP = 17
QK_GAPS = {12: 0, 14: 1, 18: 2}

PROJ_ACT = list(range(0, 23)) + list(range(31, 35))
PROJ_DVE = list(range(23, 31))


def narrow(c):
    return c in (C_BB, C_BB + 1, C_PP, C_PP + 1)


def half_at(layer, c, half):
    return layer * (2 * CHUNKS) + (2 * c + half + 1 + 2 * RING)


def scores_item(g):
    if g < 2 * B_ITEMS and g % 2 == 0:
        return g // 2
    return B_ITEMS + g - A_GAP if A_GAP <= g < A_GAP + A_ITEMS else None


def transpose_item(g):
    if g < 2 * B_ITEMS and g % 2 == 1:
        return g // 2
    return B_ITEMS + g - A_GAP - 2 if A_GAP + 2 <= g < A_GAP + 2 + A_ITEMS else None


def value_item(g):
    if 3 <= g < 2 * B_ITEMS + 3 and g % 2 == 1:
        return (g - 3) // 2
    return B_ITEMS + g - A_GAP - 3 if A_GAP + 3 <= g < A_GAP + 3 + A_ITEMS else None


def build(nc, x, p, ln_emb_g, ln_emb_b, w_in, b_gate, q_norm_g, k_norm_g, w_branch_a, w_branch_b,
          w_out, ln1_g, ln1_b, w_ffn_in, w_ffn_out, ln2_g, ln2_b, w_ple_proj, w_ple_gate,
          dist_table, rope_table, identity_table, out):
    ctx = ExitStack()
    with ctx:
        def sb(name, shape, dt=F32):
            return ctx.enter_context(nc.sbuf_tensor(name, shape, dt))

        def sem(name):
            return ctx.enter_context(nc.semaphore(name))

        w_raw = sb("w_raw", [P, RING, WORDS])
        w_hi = sb("w_hi", [P, RING, WORDS], F32R)
        w_lo = sb("w_lo", [P, RING, WORDS], F32R)
        x_nat = sb("x_nat", [P, TILES, D])
        xT_hi = sb("xT_hi", [P, KT, SEQ], F32R)
        xT_lo = sb("xT_lo", [P, KT, SEQ], F32R)
        ln_gb = sb("ln_gb", [P, 2, D])
        dist = sb("dist", [P, TILES, B_GROUPS, SEQ])
        rope = sb("rope", [P, TILES, 2, HEAD])
        rope_q = sb("rope_q", [P, TILES, 2, HEAD])
        rope_k = sb("rope_k", [P, TILES, 2, HEAD])
        qk_gain = sb("qk_gain", [P, 2, HEAD])
        bias_raw = sb("bias_raw", [P, 2 * KT])
        bias_half = sb("bias_half", [P, 2 * KT])
        ident = sb("ident", [P, P])
        kqB = sb("kqB", [P, 2 * B_GROUPS * 2, SEQ])
        vB = sb("vB", [P, TILES, B_D])
        vA = sb("vA", [P, TILES, A_KVD])
        q_raw = sb("q_raw", [P, TILES, 512])
        q_sq = sb("q_sq", [P, TILES, 512])
        q_rot = sb("q_rot", [P, 2, TILES, 512])
        qAT = sb("qAT", [P, KT, SEQ])
        kAT = sb("kAT", [P, A_KV, SEQ])
        oBT_hi = sb("oBT_hi", [P, 2, SEQ], F32R)
        oBT_lo = sb("oBT_lo", [P, 2, SEQ], F32R)
        oAT_hi = sb("oAT_hi", [P, KT, SEQ], F32R)
        oAT_lo = sb("oAT_lo", [P, KT, SEQ], F32R)
        probs = sb("probs", [P, 1536])
        probsT = sb("probsT", [P, 2, 768])
        p_nat = sb("p_nat", [P, TILES, PLE])
        pT_hi = sb("pT_hi", [P, 2, SEQ], F32R)
        pT_lo = sb("pT_lo", [P, 2, SEQ], F32R)
        smax = sb("smax", [P, 4, 2])
        nbias = sb("nbias", [P, 4, 2])
        denom = sb("denom", [P, 4, 2])
        rdenom = sb("rdenom", [P, 4, 2])
        head_ms = sb("head_ms", [P, 16])
        head_ve = sb("head_ve", [P, 16])
        head_rstd = sb("head_rstd", [P, 16])
        bn = sb("bn", [P, TILES, 2, 6])
        mean_var = sb("mean_var", [P, TILES, 2])
        ln_ve = sb("ln_ve", [P, TILES])
        ln_rstd = sb("ln_rstd", [P, TILES])
        minus_half = sb("minus_half", [P, 16])

        res = qAT[:, :, :].rearrange("p k s -> p (k s)").rearrange("p (t d) -> p t d", t=TILES)
        gateB = kqB[:, 0:KT, :]
        gateA = q_rot[:, :, :, :].rearrange("p a t n -> p (a t n)").rearrange("p (k s) -> p k s", k=KT)
        ple = kqB[:, 0:KT, :].rearrange("p k s -> p (k s)").rearrange("p (t d) -> p t d", t=TILES)
        act_t = q_raw
        hid = q_sq
        hT_hi, hT_lo = oAT_hi, oAT_lo
        kBT = kqB[:, 0:6, :]
        qBT = kqB[:, 6:12, :]

        bank = [ctx.enter_context(nc.psum_tensor(f"bank{b}", [P, 512], F32)) for b in range(8)]
        acc = bank[3:7]
        ot_bank = bank[7]
        ffn_bank = [(bank[0], bank[1]), (bank[2], bank[7])]

        w_landed = [sem(f"w_landed{s}") for s in range(RING)]
        hi_split = sem("hi_split")
        lo_split = sem("lo_split")
        half_done = sem("half_done")
        const_landed = sem("const_landed")
        gb_landed = sem("gb_landed")
        small_landed = sem("small_landed")
        p_landed = sem("p_landed")
        half_set = sem("half_set")
        doubled = sem("doubled")
        head_ve_set = sem("head_ve_set")
        pool_steps = sem("pool_steps")
        dve_chain = sem("dve_chain")
        var_ready = sem("var_ready")
        rstd_ready = sem("rstd_ready")
        x_ready = sem("x_ready")
        xT_done = sem("xT_done")
        xT_hi_done = sem("xT_hi_done")
        xT_lo_done = sem("xT_lo_done")
        pT_done = sem("pT_done")
        pT_hi_done = sem("pT_hi_done")
        pT_lo_done = sem("pT_lo_done")
        proj_act = sem("proj_act")
        proj_dve = sem("proj_dve")
        sq_ready = sem("sq_ready")
        ms_ready = sem("ms_ready")
        head_rstd_ready = sem("head_rstd_ready")
        rotated = sem("rotated")
        qkT_done = sem("qkT_done")
        qkT_taken = sem("qkT_taken")
        scores_done = sem("scores_done")
        z_done = sem("z_done")
        nbias_done = sem("nbias_done")
        exp_done = sem("exp_done")
        probs_done = sem("probs_done")
        probsT_done = sem("probsT_done")
        probsT_taken = sem("probsT_taken")
        ot_done = sem("ot_done")
        ot_hi_done = sem("ot_hi_done")
        ot_lo_done = sem("ot_lo_done")
        u_done = sem("u_done")
        u_hi_done = sem("u_hi_done")
        u_lo_done = sem("u_lo_done")
        pg_tanh = sem("pg_tanh")
        pg_used = sem("pg_used")
        ff_tanh = sem("ff_tanh")
        h_done = sem("h_done")
        h_hi_done = sem("h_hi_done")
        h_lo_done = sem("h_lo_done")
        out_stored = sem("out_stored")

        def ot_place(n):
            if n < B_ITEMS:
                h, t = n // TILES, n % TILES
                rows = slice(HEAD * (h % 2), HEAD * (h % 2) + HEAD)
                cols = slice((h // 2) * SEQ + t * P, (h // 2) * SEQ + (t + 1) * P)
                return (oBT_hi[rows, h // 2, t * P:(t + 1) * P], oBT_lo[rows, h // 2, t * P:(t + 1) * P],
                        ot_bank[rows, cols])
            j = n - B_ITEMS
            rows = slice(HEAD * (j % 2), HEAD * (j % 2) + HEAD)
            cols = slice((j // 2 % 2) * SEQ, (j // 2 % 2) * SEQ + SEQ)
            return oAT_hi[rows, j // 2, :], oAT_lo[rows, j // 2, :], ot_bank[rows, cols]

        def wait_alone(eng, semaphore, value):
            value = value if isinstance(value, int) else eng.to_reg(value)
            eng.wait_ge(semaphore, 1)
            eng.wait_ge(semaphore, value)

        block = ctx.enter_context(nc.Block())

        @block.sync
        def _(sp):
            def rows(w, layer, k0, k, c0, n):
                return w[layer, k0 * P:(k0 + k) * P, bass.ds(c0, n)].rearrange("(k p) n -> p k n", p=P)

            def source(layer, c):
                if c < C_QB:
                    return rows(w_in, layer, 0, KT, KB0 + 256 * c, 256)
                if c < C_VB:
                    return rows(w_in, layer, 0, KT, QB0 + 256 * (c - C_QB), 256)
                if c < C_VB + 2:
                    return rows(w_in, layer, 4 * (c - C_VB), 4, VB0, 512)
                if c == C_VB + 2:
                    return rows(w_in, layer, 0, KT, VB0 + 512, 256)
                if c < C_QA:
                    return rows(w_in, layer, 4 * (c - C_KV), 4, KA0, 512)
                if c < C_GB:
                    return rows(w_in, layer, 4 * ((c - C_QA) % 2), 4, QA0 + 512 * ((c - C_QA) // 2), 512)
                if c < C_GA:
                    return rows(w_in, layer, 0, KT, GATE0 + D + 256 * (c - C_GB), 256)
                if c < C_BB:
                    return rows(w_in, layer, 0, KT, GATE0 + 256 * (c - C_GA), 256)
                if c < C_BA:
                    return rows(w_branch_b, layer, 0, 2, 512 * (c - C_BB), 512)
                if c < C_WO:
                    return rows(w_branch_a, layer, 0, KT, 256 * (c - C_BA), 256)
                if c < C_PP:
                    return rows(w_out, layer, 4 * ((c - C_WO) % 2), 4, 512 * ((c - C_WO) // 2), 512)
                if c < C_PG:
                    return rows(w_ple_proj, layer, 0, 2, 512 * (c - C_PP), 512)
                return rows(w_ple_gate, layer, 4 * ((c - C_PG) % 2), 4, 512 * ((c - C_PG) // 2), 512)

            def load(chunk_index, slot, src):
                k, n = src.shape[1], src.shape[2]
                wait_alone(sp, lo_split, chunk_index + 1)
                sp.dma_start(w_raw[:, slot, 0:k * n].rearrange("p (k n) -> p k n", k=k), src)\
                  .then_inc(w_landed[slot], 16)

            for c in range(AHEAD):
                load(c, c, source(0, c))
            with sp.Fori(0, DEPTH) as layer:
                for c in range(AHEAD, C_FF):
                    load(layer * CHUNKS + c, c % RING, source(layer, c))
                load(layer * CHUNKS + C_FF, C_FF % RING, rows(w_ffn_in, layer, 0, KT, 0, 256))
                load(layer * CHUNKS + C_FF + 1, (C_FF + 1) % RING, rows(w_ffn_in, layer, 0, KT, FFN, 256))
                with sp.Fori(0, FB - 1) as f:
                    at = layer * CHUNKS + f * 3 + (C_FF + 2)
                    load(at, (C_FF + 2) % RING, rows(w_ffn_in, layer, 0, KT, f * 256 + 256, 256))
                    load(at + 1, C_FF % RING, rows(w_ffn_in, layer, 0, KT, f * 256 + (FFN + 256), 256))
                    wo_rows = w_ffn_out[layer, :, :].rearrange("(b k p) n -> b p k n", k=2, p=P)
                    load(at + 2, (C_FF + 1) % RING, wo_rows[f, :, :, :])
                load(layer * CHUNKS + (CHUNKS - 1), (CHUNKS - 1) % RING,
                     rows(w_ffn_out, layer, 2 * (FB - 1), 2, 0, D))
                following = (layer + 1) % DEPTH
                for c in range(AHEAD):
                    load(layer * CHUNKS + (CHUNKS + c), c, source(following, c))
            for t in range(TILES):
                sp.wait_ge(x_ready, DEPTH * 4 + t + 1)
                sp.dma_start(out[0, t * P:(t + 1) * P, :], x_nat[:, t, :]).then_inc(out_stored, 16)
            sp.wait_ge(out_stored, 16 * TILES)

        @block.gpsimd
        def _(pool):
            pool.dma_start(res, x.rearrange("b (t p) d -> p (b t) d", p=P)).then_inc(const_landed, 16)
            pool.dma_start(ident[:, :], identity_table).then_inc(const_landed, 16)
            pool.dma_start(ln_gb[:, 0, :], ln_emb_g.rearrange("(a d) -> a d", a=1).broadcast_to((P, D)))\
                .then_inc(gb_landed, 16)
            pool.dma_start(ln_gb[:, 1, :], ln_emb_b.rearrange("(a d) -> a d", a=1).broadcast_to((P, D)))\
                .then_inc(gb_landed, 16)
            pool.dma_start(p_nat[:, :, :], p[0, 0, :, :].rearrange("(t p) d -> p t d", p=P))\
                .then_inc(p_landed, 16)
            pool.dma_start(rope[:, :, :, :], rope_table).then_inc(const_landed, 16)
            pool.dma_start(dist[:, :, :, :], dist_table).then_inc(const_landed, 16)
            nc.gpsimd.memset(minus_half[:, :], -0.5).then_inc(half_set, 1)

            def load_small(layer):
                pool.dma_start(bias_raw[:, :], b_gate[layer, :].rearrange("(k p) -> p k", p=P),
                               allow_slow_non_contiguous=True)\
                    .then_inc(small_landed, 16)
                pool.dma_start(qk_gain[:, 0, :], q_norm_g[layer, :].rearrange("(a d) -> a d", a=1)
                               .broadcast_to((P, HEAD))).then_inc(small_landed, 16)
                pool.dma_start(qk_gain[:, 1, :], k_norm_g[layer, :].rearrange("(a d) -> a d", a=1)
                               .broadcast_to((P, HEAD))).then_inc(small_landed, 16)

            def load_gb(layer, g, b):
                pool.dma_start(ln_gb[:, 0, :], g[layer, :].rearrange("(a d) -> a d", a=1)
                               .broadcast_to((P, D))).then_inc(gb_landed, 16)
                pool.dma_start(ln_gb[:, 1, :], b[layer, :].rearrange("(a d) -> a d", a=1)
                               .broadcast_to((P, D))).then_inc(gb_landed, 16)

            def ln_power(n, chain):
                wait_alone(pool, var_ready, n)
                nc.gpsimd.tensor_scalar(ln_ve[:, :], mean_var[:, :, 1], 4 * LN_EPS, None, ALU.add)\
                    .then_inc(pool_steps, 1)
                pool.wait_ge(pool_steps, chain)
                nc.gpsimd.tensor_tensor(ln_rstd[:, :], ln_ve[:, :], minus_half[:, 0:TILES], ALU.pow)\
                    .then_inc(rstd_ready, 1)

            load_small(0)
            pool.wait_ge(half_set, 1)
            with pool.Fori(0, DEPTH) as layer:
                following = (layer + 1) % DEPTH
                chain = layer * POOL_STEPS
                ln_power(layer * 4 + 2, chain + 1)
                pool.wait_ge(small_landed, layer * 48 + 48)
                pool.wait_ge(const_landed, 64)
                wait_alone(pool, x_ready, layer * 4 + 2)
                load_gb(layer, ln1_g, ln1_b)
                nc.gpsimd.tensor_scalar(bias_half[:, :], bias_raw[:, :], 0.5, None, ALU.mult)\
                    .then_inc(pool_steps, 1)
                for part, table in ((0, rope_q), (1, rope_k)):
                    for t in range(TILES):
                        nc.gpsimd.tensor_tensor(table[:, t, 0, :], rope[:, t, 0, :], qk_gain[:, part, :],
                                                ALU.mult).then_inc(pool_steps, 1)
                        for half in range(2):
                            def halves(ap, h):
                                return ap.rearrange("p (a h j) -> p a h j", a=2, h=2)[:, :, h, :]
                            nc.gpsimd.tensor_tensor(halves(table[:, t, 1, :], half),
                                                    halves(rope[:, t, 1, :], half),
                                                    halves(qk_gain[:, part, :], 1 - half),
                                                    ALU.mult).then_inc(pool_steps, 1)
                wait_alone(pool, pool_steps, chain + TABLES)
                load_small(following)
                wait_alone(pool, pT_done, layer + 1)
                pool.dma_start(p_nat[:, :, :], p[following, 0, :, :].rearrange("(t p) d -> p t d", p=P))\
                    .then_inc(p_landed, 16)
                for slab in range(3):
                    n = 8 if slab == 0 else 16
                    wait_alone(pool, ms_ready, layer * 3 + (slab + 1))
                    nc.gpsimd.tensor_scalar(head_ve[:, 0:n], head_ms[:, 0:n], 1.0 / HEAD, RMS_EPS,
                                            ALU.mult, ALU.add).then_inc(head_ve_set, 1)
                    wait_alone(pool, head_ve_set, layer * 3 + (slab + 1))
                    nc.gpsimd.tensor_tensor(head_rstd[:, 0:n], head_ve[:, 0:n], minus_half[:, 0:n],
                                            ALU.pow).then_inc(head_rstd_ready, 1)
                ln_power(layer * 4 + 4, chain + POOL_STEPS)
                wait_alone(pool, x_ready, layer * 4 + 4)
                load_gb(layer, ln2_g, ln2_b)
            ln_power(DEPTH * 4 + 2, DEPTH * POOL_STEPS + 1)

        @block.scalar
        def _(act):
            def split_hi(index, landed, slot, words=WORDS):
                act.wait_ge(w_landed[slot], landed)
                act.wait_ge(half_done, index * 2 + 2)
                nc.scalar.activation(w_hi[:, slot, 0:words], w_raw[:, slot, 0:words], ACT.Copy)\
                    .then_inc(hi_split, 1)

            def x_transposes(n, banks):
                for t in range(TILES):
                    for half in range(2):
                        act.wait_ge(xT_done, n + (2 * t + half + 1))
                        src = banks[2 * t + half]
                        nc.scalar.activation(xT_hi[:, 4 * half:4 * half + 4, t * P:(t + 1) * P],
                                             src[:, :].rearrange("p (k s) -> p k s", k=4), ACT.Copy)\
                            .then_inc(xT_hi_done, 1)

            def take(layer, c, half, dst, src, last=True):
                act.wait_ge(half_done, half_at(layer, c, half))
                i = nc.scalar.activation(dst, src, ACT.Copy)
                if last:
                    i.then_inc(proj_act, 1)

            def slab(layer, s):
                w = 256 if s == 0 else 512
                c, u = C_KV + 1 + 2 * s, C_KV + 2 * s
                if s:
                    act.wait_ge(rotated, layer * 3 + s)
                for t in range(TILES):
                    src = bank[(u + t) % 3]
                    if s == 0:
                        take(layer, c, t, q_raw[:, t, 0:256], src[:, 0:256], last=False)
                        take(layer, c, t, vA[:, t, :], src[:, 256:512])
                    else:
                        take(layer, c, t, q_raw[:, t, :], src[:, :])
                act.wait_ge(proj_act, layer * len(PROJ_ACT) + (u + TILES))
                nc.scalar.activation(q_sq[:, :, 0:w], q_raw[:, :, 0:w], ACT.Square).then_inc(sq_ready, 1)

            def gap(layer, g):
                if g in QK_GAPS:
                    s = QK_GAPS[g]
                    for t in range(TILES):
                        act.wait_ge(qkT_done, layer * 6 + (2 * s + t + 1))
                        dst = kAT[:, :, t * P:(t + 1) * P] if s == 0 else \
                            qAT[:, 4 * (s - 1):4 * s, t * P:(t + 1) * P]
                        nc.scalar.activation(dst, bank[5 + t][:, :].rearrange("p (k s) -> p k s", k=4),
                                             ACT.Copy).then_inc(qkT_taken, 1)
                n = transpose_item(g)
                if n is not None:
                    act.wait_ge(probsT_done, layer * ITEMS + (n + 1))
                    if n >= 2:
                        act.wait_ge(ot_done, layer * ITEMS + (n - 1))
                    if n < B_ITEMS:
                        nc.scalar.activation(probsT[:, n % 2, 0:512], bank[5][:, :], ACT.Copy)
                        nc.scalar.activation(probsT[:, n % 2, 512:768], bank[6][:, 0:256], ACT.Copy)\
                            .then_inc(probsT_taken, 1)
                    else:
                        nc.scalar.activation(probsT[:, n % 2, 0:512], bank[5 + n % 2][:, :], ACT.Copy)\
                            .then_inc(probsT_taken, 1)
                n = value_item(g)
                if n is not None:
                    act.wait_ge(ot_done, layer * ITEMS + (n + 1))
                    hi, _, src = ot_place(n)
                    nc.scalar.activation(hi, src, ACT.Copy).then_inc(ot_hi_done, 1)
                n = scores_item(g)
                if n is not None:
                    act.wait_ge(nbias_done, layer * ITEMS + (n + 1))
                    if n < B_ITEMS:
                        z = probs[:, (n % 2) * 768:(n % 2 + 1) * 768]
                        nc.scalar.activation(z, z, ACT.Exp, bias=nbias[:, n % 4, 0:1], scale=SCALE,
                                             accum_out=denom[:, n % 4, 0:1]).then_inc(exp_done, 1)
                    else:
                        j = n - B_ITEMS
                        for t in range(TILES):
                            e = nc.scalar.activation(
                                probs[:, (j % 3) * 512 + t * SEQ:(j % 3) * 512 + (t + 1) * SEQ],
                                bank[3 + j % 2][:, t * SEQ:(t + 1) * SEQ], ACT.Exp,
                                bias=nbias[:, n % 4, t:t + 1], scale=SCALE,
                                accum_out=denom[:, n % 4, t:t + 1])
                        e.then_inc(exp_done, 1)

            for c in range(AHEAD):
                split_hi(c, 16, c)
            with act.Fori(0, DEPTH) as layer:
                act.wait_ge(pT_done, layer + 1)
                nc.scalar.activation(pT_hi[:, :, :], bank[2][:, :].rearrange("p (k s) -> p k s", k=2),
                                     ACT.Copy).then_inc(pT_hi_done, 1)
                x_transposes(layer * 8, (bank[0], bank[1], bank[2], bank[7]))

                def ahead(c):
                    split_hi(layer * CHUNKS + (c + AHEAD), layer * (16 * CHUNKS // RING)
                             + 16 * ((c + AHEAD) // RING + 1), (c + AHEAD) % RING,
                             WORDS // 2 if narrow(c + AHEAD) else WORDS)

                for c in range(C_FF):
                    ahead(c)
                    if c < C_VB:
                        dst = (kBT if c < C_QB else qBT)[:, 2 * (c % 3):2 * (c % 3) + 2, :]
                        take(layer, c, 1, dst, bank[c % 3][:, :].rearrange("p (k s) -> p k s", k=2))
                    for half in range(2):
                        if c == C_VB + 1:
                            take(layer, c, half, vB[:, half, 0:512], bank[(C_VB + half) % 3][:, :])
                        if c == C_VB + 2 and half == 1:
                            take(layer, c, 1, vB[:, :, 512:768], bank[2][:, :].rearrange("p (t n) -> p t n", t=TILES))
                        if half == 1 and c in (C_KV + 1, C_QA + 1, C_QA + 3):
                            slab(layer, (c - C_KV - 1) // 2)
                        if half == 1 and C_GB <= c < C_BB:
                            if c == C_GB:
                                act.wait_ge(pool_steps, layer * POOL_STEPS + TABLES)
                            q = (c - C_GB) % 4
                            dst, b0 = (gateB, KT) if c < C_GA else (gateA, 0)
                            act.wait_ge(half_done, half_at(layer, c, 1))
                            for b in range(2):
                                i = nc.scalar.activation(dst[:, 2 * q + b, :], bank[c % 3][:, b * SEQ:(b + 1) * SEQ],
                                                         ACT.Tanh, scale=0.5,
                                                         bias=bias_half[:, b0 + 2 * q + b:b0 + 2 * q + b + 1])
                            i.then_inc(proj_act, 1)
                        if GAP_CHUNK <= c < C_BA:
                            gap(layer, 2 * (c - GAP_CHUNK) + half)
                    if C_BA <= c < C_WO:
                        q = c - C_BA
                        act.wait_ge(u_done, layer * 4 + (q + 1))
                        nc.scalar.activation(xT_hi[:, 2 * q:2 * q + 2, :], gateA[:, 2 * q:2 * q + 2, :],
                                             ACT.Copy).then_inc(u_hi_done, 1)
                    if C_PP <= c < C_PG:
                        for t in range(TILES):
                            u = 31 + 2 * (c - C_PP) + t
                            take(layer, c, t, ple[:, t, (c - C_PP) * 512:(c - C_PP + 1) * 512], bank[u % 3][:, :])
                        if c == C_PG - 1:
                            x_transposes(layer * 8 + 4, (bank[2], bank[0], bank[1], bank[7]))
                    if C_PG <= c and (c - C_PG) % 2 == 1:
                        h = (c - C_PG) // 2
                        for t in range(TILES):
                            n = 2 * h + t
                            act.wait_ge(half_done, half_at(layer, c, t))
                            if n >= 2:
                                act.wait_ge(pg_used, layer * 4 + (n - 1))
                            nc.scalar.activation(act_t[:, n % 2, :], acc[2 * t + h][:, :], ACT.Tanh, scale=0.5)\
                                .then_inc(pg_tanh, 1)

                def ffn_tanh(gate_chunk, b):
                    act.wait_ge(half_done, half_at(layer, 0, 1) + gate_chunk * 2)
                    nc.scalar.activation(act_t[:, b, :], ffn_bank[b][0][:, :], ACT.Tanh, scale=0.5)\
                        .then_inc(ff_tanh, 1)

                def hidden_hi(fi, b):
                    act.wait_ge(h_done, layer * FB + fi + 1)
                    nc.scalar.activation(hT_hi[:, 2 * b:2 * b + 2, :], hid[:, b, :].rearrange("p (k s) -> p k s", k=2),
                                         ACT.Copy).then_inc(h_hi_done, 1)

                def ahead_ffn(fi, j, slot):
                    split_hi(layer * CHUNKS + fi * 3 + (C_FF + 4 + j),
                             layer * (16 * CHUNKS // RING) + fi * 16 + 16 * ((C_FF + 4 + j) // RING + 1), slot)

                ahead(C_FF)
                ahead(C_FF + 1)
                act.wait_ge(pg_used, layer * 4 + 4)
                ffn_tanh(C_FF, 0)
                hidden_hi(0, 0)
                with act.Fori(0, (FB - 1) // 2) as pair:
                    for b in range(2):
                        f = pair * 2 + b
                        ahead_ffn(f, 0, (C_FF + 4) % RING)
                        ahead_ffn(f, 1, (C_FF + 5) % RING)
                        ffn_tanh(f * 3 + (C_FF + 2), 1 - b)
                        ahead_ffn(f, 2, (C_FF + 6) % RING)
                        hidden_hi(f + 1, 1 - b)
                ahead(CHUNKS - 1)

        @block.vector
        def _(dve):
            DC = 400
            used = [0]
            base = [0]

            def link(ins):
                used[0] += 1
                ins.then_inc(dve_chain, 1)
                dve.wait_ge(dve_chain, base[0] + used[0])

            def split_lo(index, slot, words=WORDS):
                dve.wait_ge(hi_split, index + 1)
                nc.vector.tensor_tensor(w_lo[:, slot, 0:words], w_raw[:, slot, 0:words],
                                        w_hi[:, slot, 0:words].bitcast(F32),
                                        ALU.subtract).then_inc(lo_split, 1)

            def layer_norm(gb, n_rstd, dst):
                for t in range(TILES):
                    nc.vector.bn_stats(bn[:, t, 0, :], res[:, t, 0:512])
                    used[0] += 1
                    nc.vector.bn_stats(bn[:, t, 1, :], res[:, t, 512:1024]).then_inc(dve_chain, 1)
                    wait_alone(dve, dve_chain, base[0] + used[0])
                    nc.vector.bn_aggr(mean_var[:, t, :], bn[:, t, :, :]).then_inc(var_ready, 1)
                dve.wait_ge(gb_landed, gb)
                dve.wait_ge(var_ready, n_rstd * 2)
                for t in range(TILES):
                    link(nc.vector.scalar_tensor_tensor(dst[:, t, :], res[:, t, :], mean_var[:, t, 0:1],
                                                        ln_gb[:, 0, :], ALU.subtract, ALU.mult))
                dve.wait_ge(rstd_ready, n_rstd)
                for t in range(TILES):
                    nc.vector.scalar_tensor_tensor(dst[:, t, :], dst[:, t, :], ln_rstd[:, t:t + 1],
                                                   ln_gb[:, 1, :], ALU.mult, ALU.add).then_inc(x_ready, 1)

            def x_transposes(n, banks):
                for t in range(TILES):
                    for half in range(2):
                        dve.wait_ge(xT_hi_done, n + (2 * t + half + 1))
                        at = (slice(None), slice(4 * half, 4 * half + 4), slice(t * P, (t + 1) * P))
                        nc.vector.tensor_tensor(xT_lo[at], banks[2 * t + half][:, :].rearrange("p (k s) -> p k s", k=4),
                                                xT_hi[at].bitcast(F32), ALU.subtract).then_inc(xT_lo_done, 1)

            def rotate(layer, s):
                w = 256 if s == 0 else 512
                nh = w // HEAD
                raw = q_raw[:, :, 0:w].rearrange("p t (h d) -> p t h d", d=HEAD)
                sq = q_sq[:, :, 0:w].rearrange("p t (h d) -> p t h d", d=HEAD)
                table = rope_k if s == 0 else rope_q
                dve.wait_ge(sq_ready, layer * 3 + (s + 1))
                if s == 0:
                    dve.wait_ge(pool_steps, layer * POOL_STEPS + TABLES)
                ms = head_ms[:, 0:2 * nh].rearrange("p (t h) -> p t h", t=TILES)
                nc.vector.tensor_reduce(ms, sq, AX_X, ALU.add).then_inc(ms_ready, 1)
                dve.wait_ge(head_rstd_ready, layer * 3 + (s + 1))
                rs = head_rstd[:, 0:2 * nh].rearrange("p (t h) -> p t h", t=TILES).unsqueeze(3)\
                    .broadcast_to((P, TILES, nh, HEAD))
                link(nc.vector.tensor_tensor(raw, raw, rs, ALU.mult))
                for t in range(TILES):
                    for half in range(2):
                        def part(ap, h):
                            return ap.rearrange("p h (a b j) -> p h a b j", a=2, b=2)[:, :, :, h, :]
                        sine = table[:, t, 1, :].rearrange("p (a b j) -> p a b j", a=2, b=2)[:, :, half, :]\
                            .unsqueeze(1).broadcast_to((P, nh, 2, 16))
                        i = nc.vector.tensor_tensor(part(sq[:, t, :, :], half),
                                                    part(raw[:, t, :, :], 1 - half), sine, ALU.mult)
                link(i)
                cosine = table[:, :, 0, :].unsqueeze(2).broadcast_to((P, TILES, nh, HEAD))
                link(nc.vector.tensor_tensor(raw, raw, cosine, ALU.mult))
                if s == 0:
                    for t in range(TILES):
                        twice = (P, nh, 2, HEAD)
                        i = nc.vector.tensor_tensor(
                            q_rot[:, 0, t, :].rearrange("p (h c d) -> p h c d", c=2, d=HEAD),
                            raw[:, t, :, :].unsqueeze(2).broadcast_to(twice),
                            sq[:, t, :, :].unsqueeze(2).broadcast_to(twice), ALU.add)
                    i.then_inc(rotated, 1)
                else:
                    if s == 2:
                        dve.wait_ge(qkT_done, layer * 6 + 2)
                    nc.vector.tensor_tensor(q_rot[:, s % 2, :, :], q_raw[:, :, :], q_sq[:, :, :], ALU.add)\
                        .then_inc(rotated, 1)

            def normalise(layer, n):
                dve.wait_ge(exp_done, layer * ITEMS + (n + 1))
                if n < B_ITEMS:
                    link(nc.vector.reciprocal(rdenom[:, n % 4, 0:1], denom[:, n % 4, 0:1]))
                    z = probs[:, (n % 2) * 768:(n % 2 + 1) * 768]
                    nc.vector.tensor_scalar(z, z, rdenom[:, n % 4, 0:1], None, ALU.mult).then_inc(probs_done, 1)
                else:
                    j = n - B_ITEMS
                    link(nc.vector.reciprocal(rdenom[:, n % 4, :], denom[:, n % 4, :]))
                    for t in range(TILES):
                        z = probs[:, (j % 3) * 512 + t * SEQ:(j % 3) * 512 + (t + 1) * SEQ]
                        i = nc.vector.tensor_scalar(z, z, rdenom[:, n % 4, t:t + 1], None, ALU.mult)
                    i.then_inc(probs_done, 1)

            def gap(layer, g):
                n = scores_item(g - 1)
                if n is not None:
                    normalise(layer, n)
                n = scores_item(g)
                if n is not None:
                    dve.wait_ge(scores_done, layer * ITEMS + (n + 1))
                    if n < B_ITEMS:
                        h, t = n // TILES, n % TILES
                        if n >= 2:
                            dve.wait_ge(probsT_done, layer * ITEMS + (n - 1))
                        z = probs[:, (n % 2) * 768:(n % 2 + 1) * 768]
                        for gr in range(B_GROUPS):
                            s = bank[3 + gr // 2][:, (gr % 2) * SEQ:(gr % 2 + 1) * SEQ]
                            i = nc.vector.scalar_tensor_tensor(
                                z[:, gr * SEQ:(gr + 1) * SEQ], dist[:, t, gr, :],
                                SLOPE[gr * B_PER_GROUP + h] / SCALE, s, ALU.mult, ALU.add)
                        i.then_inc(z_done, 1)
                        dve.wait_ge(z_done, layer * B_ITEMS + (n + 1))
                        link(nc.vector.reduce_max(smax[:, n % 4, 0:1], z, AX_X))
                        nc.vector.tensor_scalar(nbias[:, n % 4, 0:1], smax[:, n % 4, 0:1], -SCALE, None,
                                                ALU.mult).then_inc(nbias_done, 1)
                    else:
                        j = n - B_ITEMS
                        dve.wait_ge(probsT_done, layer * ITEMS + (n - 2 if j >= 3 else B_ITEMS))
                        link(nc.vector.reduce_max(smax[:, n % 4, :], bank[3 + j % 2][:, :]
                                                  .rearrange("p (t s) -> p t s", t=TILES), AX_X))
                        nc.vector.tensor_scalar(nbias[:, n % 4, :], smax[:, n % 4, :], -SCALE, None,
                                                ALU.mult).then_inc(nbias_done, 1)
                n = value_item(g)
                if n is not None:
                    hi, lo, src = ot_place(n)
                    dve.wait_ge(ot_hi_done, layer * ITEMS + (n + 1))
                    nc.vector.tensor_tensor(lo, src, hi.bitcast(F32), ALU.subtract).then_inc(ot_lo_done, 1)

            dve.sem_inc(lo_split, RING)
            dve.wait_ge(const_landed, 64)
            link(nc.vector.tensor_scalar(res, res, 2.0, None, ALU.mult))
            for c in range(AHEAD):
                split_lo(c, c)
            start = used[0]
            with dve.Fori(0, DEPTH) as layer:
                used[0] = 0
                base[0] = layer * DC + start
                layer_norm(layer * 64 + 32, layer * 2 + 1, x_nat)
                dve.wait_ge(pT_hi_done, layer + 1)
                nc.vector.tensor_tensor(pT_lo[:, :, :], bank[2][:, :].rearrange("p (k s) -> p k s", k=2),
                                        pT_hi[:, :, :].bitcast(F32), ALU.subtract).then_inc(pT_lo_done, 1)
                x_transposes(layer * 8, (bank[0], bank[1], bank[2], bank[7]))

                def ahead(c):
                    split_lo(layer * CHUNKS + (c + AHEAD), (c + AHEAD) % RING,
                             WORDS // 2 if narrow(c + AHEAD) else WORDS)

                for c in range(C_FF):
                    ahead(c)
                    for half in range(2):
                        if GAP_CHUNK <= c < C_BA:
                            gap(layer, 2 * (c - GAP_CHUNK) + half)
                        if C_BB <= c < C_BA:
                            u = 23 + 2 * (c - C_BB) + half
                            q = 2 * (c - C_BB) + half
                            if q == 0:
                                dve.wait_ge(proj_act, layer * len(PROJ_ACT) + 23)
                            dve.wait_ge(half_done, half_at(layer, c, half))
                            nc.vector.scalar_tensor_tensor(
                                gateB[:, 2 * q:2 * q + 2, :], gateB[:, 2 * q:2 * q + 2, :], 1.0,
                                bank[u % 3][:, :].rearrange("p (k s) -> p k s", k=2), ALU.add, ALU.mult)\
                                .then_inc(proj_dve, 1)
                        if half == 1 and c in (C_KV + 1, C_QA + 1, C_QA + 3):
                            rotate(layer, (c - C_KV - 1) // 2)
                    if C_BA <= c < C_WO:
                        q = c - C_BA
                        u = 27 + q
                        ga = gateA[:, 2 * q:2 * q + 2, :]
                        dve.wait_ge(half_done, half_at(layer, c, 1))
                        nc.vector.scalar_tensor_tensor(ga, ga, 1.0, bank[u % 3][:, :]
                                                       .rearrange("p (k s) -> p k s", k=2), ALU.add, ALU.mult)\
                            .then_inc(proj_dve, 1)
                        dve.wait_ge(proj_dve, layer * len(PROJ_DVE) + (5 + q))
                        nc.vector.tensor_tensor(ga, ga, gateB[:, 2 * q:2 * q + 2, :], ALU.add).then_inc(u_done, 1)
                        dve.wait_ge(u_hi_done, layer * 4 + (q + 1))
                        nc.vector.tensor_tensor(xT_lo[:, 2 * q:2 * q + 2, :], ga,
                                                xT_hi[:, 2 * q:2 * q + 2, :].bitcast(F32), ALU.subtract)\
                            .then_inc(u_lo_done, 1)
                    if C_WO <= c < C_PP and (c - C_WO) % 2 == 1:
                        h = (c - C_WO) // 2
                        for t in range(TILES):
                            dve.wait_ge(half_done, half_at(layer, c, t))
                            cols = slice(h * 512, (h + 1) * 512)
                            i = nc.vector.scalar_tensor_tensor(res[:, t, cols], x_nat[:, t, cols], 2 * ALPHA,
                                                               acc[2 * t + h][:, :], ALU.mult, ALU.add)
                        link(i)
                    if c == C_PG - 1:
                        layer_norm(layer * 64 + 64, layer * 2 + 2, x_nat)
                        x_transposes(layer * 8 + 4, (bank[2], bank[0], bank[1], bank[7]))
                    if C_PG <= c and (c - C_PG) % 2 == 1:
                        h = (c - C_PG) // 2
                        for t in range(TILES):
                            n = 2 * h + t
                            cols = slice(h * 512, (h + 1) * 512)
                            dve.wait_ge(pg_tanh, layer * 4 + (n + 1))
                            if n == 0:
                                dve.wait_ge(proj_act, layer * len(PROJ_ACT) + len(PROJ_ACT))
                                dve.wait_ge(x_ready, layer * 4 + 4)
                            nc.vector.scalar_tensor_tensor(ple[:, t, cols], act_t[:, n % 2, :], 1.0,
                                                           ple[:, t, cols], ALU.add, ALU.mult)\
                                .then_inc(pg_used, 1)
                            dve.wait_ge(pg_used, layer * 4 + (n + 1))
                            link(nc.vector.scalar_tensor_tensor(res[:, t, cols], x_nat[:, t, cols], 2 * ALPHA,
                                                                ple[:, t, cols], ALU.mult, ALU.add))

                def hidden(fi, up_chunk, b):
                    dve.wait_ge(ff_tanh, layer * FB + fi + 1)
                    dve.wait_ge(half_done, half_at(layer, 0, 1) + up_chunk * 2)
                    link(nc.vector.scalar_tensor_tensor(hid[:, b, :], act_t[:, b, :], 1.0, ffn_bank[b][0][:, :],
                                                        ALU.add, ALU.mult))
                    nc.vector.tensor_tensor(hid[:, b, :], hid[:, b, :], ffn_bank[b][1][:, :], ALU.mult)\
                        .then_inc(h_done, 1)

                def hidden_lo(fi, b):
                    dve.wait_ge(h_hi_done, layer * FB + fi + 1)
                    nc.vector.tensor_tensor(hT_lo[:, 2 * b:2 * b + 2, :], hid[:, b, :].rearrange("p (k s) -> p k s", k=2),
                                            hT_hi[:, 2 * b:2 * b + 2, :].bitcast(F32), ALU.subtract)\
                        .then_inc(h_lo_done, 1)

                ahead(C_FF)
                ahead(C_FF + 1)
                hidden(0, C_FF + 1, 0)
                hidden_lo(0, 0)
                before = used[0]
                with dve.Fori(0, (FB - 1) // 2) as pair:
                    base[0] = layer * DC + pair * 2 + start
                    for b in range(2):
                        f = pair * 2 + b
                        at = layer * CHUNKS + f * 3 + (C_FF + 4)
                        split_lo(at, (C_FF + 4) % RING)
                        split_lo(at + 1, (C_FF + 5) % RING)
                        hidden(f + 1, f * 3 + (C_FF + 3), 1 - b)
                        split_lo(at + 2, (C_FF + 6) % RING)
                        hidden_lo(f + 1, 1 - b)
                assert used[0] == before + 2
                used[0] = before + FB - 1
                base[0] = layer * DC + start
                ahead(CHUNKS - 1)
                for t in range(TILES):
                    dve.wait_ge(half_done, half_at(layer, CHUNKS - 1, t))
                    for h in range(2):
                        cols = slice(h * 512, (h + 1) * 512)
                        i = nc.vector.tensor_tensor(res[:, t, cols], res[:, t, cols], acc[2 * t + h][:, :], ALU.add)
                link(i)
                assert used[0] < DC
                dve.sem_inc(dve_chain, DC - used[0])
            used[0] = 0
            base[0] = DEPTH * DC + start
            layer_norm(DEPTH * 64 + 32, 2 * DEPTH + 1, x_nat)

        @block.tensor
        def _(pe):
            def product(dst, l_hi, l_lo, r_hi, r_lo, start, stop):
                nc.tensor.matmul(dst, l_hi, r_hi, start=start, stop=False)
                nc.tensor.matmul(dst, l_hi, r_lo, start=False, stop=False)
                return nc.tensor.matmul(dst, l_lo, r_hi, start=False, stop=stop)

            def weights(layer, c):
                pe.wait_ge(lo_split, layer * CHUNKS + (c + 1 + RING))

            def chunk(slot, k, n):
                return [w[:, slot, 0:k * n].rearrange("p (k n) -> p k n", k=k) for w in (w_hi, w_lo)]

            def stationary(slot, k, n, block_, dst, r_hi, r_lo):
                hi, lo = chunk(slot, k, n)
                cols = slice(block_ * P, (block_ + 1) * P)
                for kt in range(k):
                    i = product(dst, hi[:, kt, cols], lo[:, kt, cols], r_hi[:, kt, :], r_lo[:, kt, :],
                                kt == 0, kt == k - 1)
                return i

            def moving(slot, k, n, cols, dst, l_hi, l_lo, k0, t, start, stop):
                hi, lo = chunk(slot, k, n)
                rows = slice(t * P, (t + 1) * P)
                for kt in range(k):
                    i = product(dst, l_hi[:, k0 + kt, rows], l_lo[:, k0 + kt, rows], hi[:, kt, cols],
                                lo[:, kt, cols], start and kt == 0, stop and kt == k - 1)
                return i

            def bank_free(layer, use):
                before = use - 3
                if before < 0:
                    return
                if before in PROJ_ACT:
                    pe.wait_ge(proj_act, layer * len(PROJ_ACT) + (PROJ_ACT.index(before) + 1))
                else:
                    pe.wait_ge(proj_dve, layer * len(PROJ_DVE) + (PROJ_DVE.index(before) + 1))

            def x_transposes(n, banks):
                for t in range(TILES):
                    pe.wait_ge(x_ready, n + (t + 1))
                    for half in range(2):
                        for k in range(4):
                            kt = 4 * half + k
                            i = nc.tensor.transpose(banks[2 * t + half][:, k * P:(k + 1) * P],
                                                    x_nat[:, t, kt * P:(kt + 1) * P], ident[:, :])
                        i.then_inc(xT_done, 1)

            def gap(layer, g):
                n = scores_item(g)
                if n is not None:
                    if n == 0:
                        pe.wait_ge(proj_act, layer * len(PROJ_ACT) + C_VB)
                    elif n <= B_ITEMS:
                        pe.wait_ge(z_done, layer * B_ITEMS + n)
                    elif n >= B_ITEMS + 2:
                        pe.wait_ge(exp_done, layer * ITEMS + (n - 1))
                    if n < B_ITEMS:
                        h, t = n // TILES, n % TILES
                        rows = slice(HEAD * (h % 2), HEAD * (h % 2) + HEAD)
                        for gr in range(B_GROUPS):
                            i = nc.tensor.matmul(bank[3 + gr // 2][:, (gr % 2) * SEQ:(gr % 2 + 1) * SEQ],
                                                 qBT[rows, 2 * gr + h // 2, t * P:(t + 1) * P],
                                                 kBT[rows, 2 * gr + h // 2, :], start=True, stop=True)
                    else:
                        j = n - B_ITEMS
                        if j == 0:
                            pe.wait_ge(qkT_taken, layer * 6 + 4)
                        if j == 8:
                            pe.wait_ge(qkT_taken, layer * 6 + 6)
                        rows = slice(HEAD * (j % 2), HEAD * (j % 2) + HEAD)
                        for t in range(TILES):
                            i = nc.tensor.matmul(bank[3 + j % 2][:, t * SEQ:(t + 1) * SEQ],
                                                 qAT[rows, j // 2, t * P:(t + 1) * P], kAT[rows, j // 4, :],
                                                 start=True, stop=True)
                    i.then_inc(scores_done, 1)
                if g in QK_GAPS:
                    s = QK_GAPS[g]
                    pe.wait_ge(rotated, layer * 3 + (s + 1))
                    n = {12: 6, 14: 7, 18: 8}[g]
                    pe.wait_ge(probsT_taken, layer * ITEMS + n)
                    for t in range(TILES):
                        for k in range(4):
                            i = nc.tensor.transpose(bank[5 + t][:, k * P:(k + 1) * P],
                                                    q_rot[:, s % 2, t, k * P:(k + 1) * P], ident[:, :])
                        i.then_inc(qkT_done, 1)
                n = transpose_item(g)
                if n is not None:
                    pe.wait_ge(probs_done, layer * ITEMS + (n + 1))
                    if 0 < n < B_ITEMS:
                        pe.wait_ge(probsT_taken, layer * ITEMS + n)
                    elif n >= B_ITEMS + 2:
                        pe.wait_ge(probsT_taken, layer * ITEMS + (n - 1))
                    if n in (6, 7, B_ITEMS):
                        pe.wait_ge(qkT_taken, layer * 6 + {6: 2, 7: 4, B_ITEMS: 6}[n])
                    if n < B_ITEMS:
                        for gr in range(B_GROUPS):
                            for kt in range(2):
                                at = (gr * 2 + kt) * P
                                i = nc.tensor.transpose(bank[5 + gr // 2][:, at % 512:at % 512 + P],
                                                        probs[:, (n % 2) * 768 + at:(n % 2) * 768 + at + P],
                                                        ident[:, :])
                    else:
                        j = n - B_ITEMS
                        for kt in range(2):
                            for t in range(TILES):
                                at = (j % 3) * 512 + t * SEQ + kt * P
                                i = nc.tensor.transpose(bank[5 + n % 2][:, kt * SEQ + t * P:kt * SEQ + (t + 1) * P],
                                                        probs[:, at:at + P], ident[:, :])
                    i.then_inc(probsT_done, 1)
                n = value_item(g)
                if n is not None:
                    pe.wait_ge(probsT_taken, layer * ITEMS + (n + 1))
                    if n > 0:
                        pe.wait_ge(ot_lo_done, layer * ITEMS + (n if n <= B_ITEMS else n - 1))
                    _, _, dst = ot_place(n)
                    if n < B_ITEMS:
                        h = n // TILES
                        if n == 0:
                            pe.wait_ge(proj_act, layer * len(PROJ_ACT) + 9)
                        for gr in range(B_GROUPS):
                            for kt in range(2):
                                i = nc.tensor.matmul(dst, vB[:, kt, (gr * B_PER_GROUP + h) * HEAD:
                                                             (gr * B_PER_GROUP + h + 1) * HEAD],
                                                     probsT[:, n % 2, (gr * 2 + kt) * P:(gr * 2 + kt + 1) * P],
                                                     start=gr == 0 and kt == 0, stop=gr == 2 and kt == 1)
                    else:
                        j = n - B_ITEMS
                        for kt in range(2):
                            i = nc.tensor.matmul(dst, vA[:, kt, (j // 4) * HEAD:(j // 4 + 1) * HEAD],
                                                 probsT[:, n % 2, kt * SEQ:(kt + 1) * SEQ],
                                                 start=kt == 0, stop=kt == 1)
                    i.then_inc(ot_done, 1)

            pe.sem_inc(half_done, 2 * RING)
            pe.wait_ge(const_landed, 64)
            with pe.Fori(0, DEPTH) as layer:
                pe.wait_ge(p_landed, layer * 16 + 16)
                for kt in range(2):
                    for t in range(TILES):
                        i = nc.tensor.transpose(bank[2][:, kt * SEQ + t * P:kt * SEQ + (t + 1) * P],
                                                p_nat[:, t, kt * P:(kt + 1) * P], ident[:, :])
                i.then_inc(pT_done, 1)
                pe.wait_ge(pT_lo_done, layer + 1)
                x_transposes(layer * 4, (bank[0], bank[1], bank[2], bank[7]))
                pe.wait_ge(xT_lo_done, layer * 8 + 4)

                for c in range(C_FF):
                    s = c % RING
                    weights(layer, c)
                    if c == C_BB:
                        pe.wait_ge(ot_lo_done, layer * ITEMS + B_ITEMS)
                    if c == C_BA:
                        pe.wait_ge(ot_lo_done, layer * ITEMS + ITEMS)
                    if c == C_WO:
                        pe.wait_ge(u_lo_done, layer * 4 + 4)
                    if c == C_PG:
                        pe.wait_ge(proj_act, layer * len(PROJ_ACT) + len(PROJ_ACT))
                        x_transposes(layer * 4 + 2, (bank[2], bank[0], bank[1], bank[7]))
                        pe.wait_ge(xT_lo_done, layer * 8 + 8)
                    for half in range(2):
                        if c < C_VB or C_GB <= c < C_BB or C_BA <= c < C_WO:
                            use = c if c < C_BB else c + 2
                            if half == 0:
                                bank_free(layer, use)
                            r = (oAT_hi, oAT_lo) if c >= C_BA else (xT_hi, xT_lo)
                            i = stationary(s, KT, 256, half, bank[use % 3][:, half * SEQ:(half + 1) * SEQ], *r)
                        elif C_BB <= c < C_BA:
                            use = 23 + 2 * (c - C_BB) + half
                            bank_free(layer, use)
                            for b in range(2):
                                i = stationary(s, 2, 512, 2 * half + b, bank[use % 3][:, b * SEQ:(b + 1) * SEQ],
                                               oBT_hi, oBT_lo)
                        elif c == C_VB + 2:
                            if half == 0:
                                bank_free(layer, 8)
                            i = moving(s, KT, 256, slice(0, 256), bank[2][:, half * SEQ:(half + 1) * SEQ],
                                       xT_hi, xT_lo, 0, half, True, True)
                        elif c < C_GB:
                            first = c in (C_VB, C_KV, C_QA, C_QA + 2)
                            use = {C_VB: 6, C_KV: 9, C_QA: 11, C_QA + 2: 13}[c if first else c - 1] + half
                            if first:
                                bank_free(layer, use)
                            i = moving(s, 4, 512, slice(0, 512), bank[use % 3][:, :], xT_hi, xT_lo,
                                       0 if first else 4, half, first, not first)
                        elif C_PP <= c < C_PG:
                            use = 31 + 2 * (c - C_PP) + half
                            bank_free(layer, use)
                            i = moving(s, 2, 512, slice(0, 512), bank[use % 3][:, :], pT_hi, pT_lo, 0, half,
                                       True, True)
                        else:
                            k, h = ((c - C_WO) if c < C_PP else (c - C_PG)) % 2, \
                                ((c - C_WO) if c < C_PP else (c - C_PG)) // 2
                            i = moving(s, 4, 512, slice(0, 512), acc[2 * half + h][:, :], xT_hi, xT_lo, 4 * k,
                                       half, k == 0, k == 1)
                        i.then_inc(half_done, 1)
                        if GAP_CHUNK <= c < C_BA:
                            gap(layer, 2 * (c - GAP_CHUNK) + half)

                def ffn_in(slot, b, part):
                    for half in range(2):
                        i = stationary(slot, KT, 256, half, ffn_bank[b][part][:, half * SEQ:(half + 1) * SEQ],
                                       xT_hi, xT_lo)
                        i.then_inc(half_done, 1)

                def ffn_out(slot, b, first, last):
                    for t in range(TILES):
                        for h in range(2):
                            i = moving(slot, 2, D, slice(h * 512, (h + 1) * 512), acc[2 * t + h][:, :], hT_hi, hT_lo,
                                       2 * b, t, first, last)
                        i.then_inc(half_done, 1)

                def ffn_step(fi, b):
                    at = layer * CHUNKS + fi * 3 + (C_FF + 3 + RING)
                    pe.wait_ge(lo_split, at)
                    ffn_in((C_FF + 2) % RING, 1 - b, 0)
                    pe.wait_ge(lo_split, at + 1)
                    ffn_in(C_FF % RING, 1 - b, 1)
                    pe.wait_ge(lo_split, at + 2)
                    pe.wait_ge(h_lo_done, layer * FB + fi + 1)

                weights(layer, C_FF)
                ffn_in(C_FF % RING, 0, 0)
                weights(layer, C_FF + 1)
                ffn_in((C_FF + 1) % RING, 0, 1)
                ffn_step(0, 0)
                pe.wait_ge(pg_used, layer * 4 + 4)
                ffn_out((C_FF + 1) % RING, 0, True, False)
                ffn_step(1, 1)
                ffn_out((C_FF + 1) % RING, 1, False, False)
                with pe.Fori(1, (FB - 1) // 2) as pair:
                    for b in range(2):
                        ffn_step(pair * 2 + b, b)
                        ffn_out((C_FF + 1) % RING, b, False, False)
                weights(layer, CHUNKS - 1)
                pe.wait_ge(h_lo_done, layer * FB + FB)
                ffn_out((CHUNKS - 1) % RING, 0, False, True)


_INS = ['x', 'p', 'ln_emb_g', 'ln_emb_b', 'w_in', 'b_gate', 'q_norm_g', 'k_norm_g', 'w_branch_a',
        'w_branch_b', 'w_out', 'ln1_g', 'ln1_b', 'w_ffn_in', 'w_ffn_out', 'ln2_g', 'ln2_b',
        'w_ple_proj', 'w_ple_gate']


def shape_tables():
    import numpy as np
    t = np.arange(SEQ)
    diff = t[None, :] - t[:, None]
    dist = np.empty((SEQ, B_GROUPS, SEQ), np.float32)
    for g, (window, dilation) in enumerate(((128, 1), (512, 4), (2048, 16))):
        reach = window // 2 // dilation * dilation
        seen = (np.abs(diff) <= reach) & (diff % dilation == 0)
        dist[:, g, :] = np.where(seen, -np.abs(diff), -1e32)
    dist = dist.reshape(TILES, P, B_GROUPS, SEQ).transpose(1, 0, 2, 3)
    grid_w, axis = 64, HEAD // 2
    inv = (np.float32(10000.0) ** (-np.arange(0, axis, 2, dtype=np.float32) / np.float32(axis))).astype(np.float32)
    row, col = (t // grid_w).astype(np.float32), (t % grid_w).astype(np.float32)
    tables = []
    for pos in (row, col):
        ang = pos[:, None] * inv[None, :]
        tables.append((np.cos(ang), np.sin(ang)))
    cos = np.concatenate([tables[0][0]] * 2 + [tables[1][0]] * 2, axis=1)
    sin = np.concatenate([-tables[0][1], tables[0][1], -tables[1][1], tables[1][1]], axis=1)
    rope = np.stack([cos, sin], axis=1).astype(np.float32).reshape(TILES, P, 2, HEAD).transpose(1, 0, 2, 3)
    return {"dist_table": np.ascontiguousarray(dist), "rope_table": np.ascontiguousarray(rope),
            "identity_table": np.eye(P, dtype=np.float32)}


def kernel(**inputs):
    import numpy as _np
    import concourse.bacc as _bacc
    from concourse import mybir as _mybir
    from concourse.bass_utils import run_bass_kernel_spmd as _run

    nc = _bacc.Bacc("TRN2", target_bir_lowering=False, num_devices=1)
    arrays, args = {}, []
    for name, a in [(n, inputs[n]) for n in _INS] + list(shape_tables().items()):
        a = _np.ascontiguousarray(a)
        arrays[f"in_{name}"] = a
        args.append(nc.dram_tensor(f"in_{name}", a.shape, _mybir.dt.from_np(a.dtype), kind="ExternalInput").ap())
    args.append(nc.dram_tensor("out_0", (1, SEQ, D), F32, kind="ExternalOutput").ap())
    build(nc, *args)
    r = _run(nc, [arrays], core_ids=[0])
    return r.results[0]["out_0"]
```

```python
import concourse.bass as bass
from concourse import mybir
from contextlib import ExitStack

F32 = mybir.dt.float32
F32R = mybir.dt.float32r
ALU = mybir.AluOpType
ACT = mybir.ActivationFunctionType
AX_X = mybir.AxisListType.X

P = 128
D = 1024
SEQ = 256
TILES = SEQ // P
KT = D // P
DEPTH = 2
HEAD = 64
A_HEADS, A_KV = 16, 4
B_GROUPS, B_PER_GROUP = 3, 4
A_Q, A_KVD, B_D = A_HEADS * HEAD, A_KV * HEAD, B_GROUPS * B_PER_GROUP * HEAD
FFN = -(-8 * D // (3 * 256)) * 256
PLE = 256
ALPHA = (2 * DEPTH) ** 0.25
LN_EPS, RMS_EPS = 1e-5, 1e-6
SCALE = HEAD ** -0.5
QA0, KA0 = 0, A_Q
QB0 = A_Q + 2 * A_KVD
KB0, VB0 = QB0 + B_D, QB0 + 2 * B_D
GATE0 = QB0 + 3 * B_D
N_B_HEADS = B_GROUPS * B_PER_GROUP
SLOPE = [2.0 ** (-8.0 * (n + 1) / N_B_HEADS) for n in range(N_B_HEADS)]

WORDS = 2048
RING = 3
C_KV = 0
C_KB, C_QB = 2, 5
C_VB = 8
C_QA = 11
C_GB, C_GA = 15, 19
C_BB, C_BA = 23, 25
C_WO, C_PP, C_PG = 29, 33, 35
C_FF = 39
FB = FFN // 256
CHUNKS = C_FF + 3 * FB
assert CHUNKS == 72 and CHUNKS % RING == 0 and C_FF % RING == 0 and FB % 2 == 1
AHEAD = 2

PAIRS = (C_KV, C_WO + 2, C_PG, CHUNKS - 2)
ORDER = []
for _c in range(CHUNKS):
    if _c in PAIRS:
        ORDER += [(_c, 0), (_c + 1, 0), (_c, 1), (_c + 1, 1)]
    elif _c - 1 not in PAIRS:
        ORDER += [(_c, 0), (_c, 1)]
assert len(ORDER) == 2 * CHUNKS

GAP_CHUNK = 8
B_ITEMS = B_PER_GROUP * TILES
A_ITEMS = A_HEADS // 2
ITEMS = B_ITEMS + A_ITEMS
VALUES = B_ITEMS // 2 + A_ITEMS
A_GAP = 2 * B_ITEMS - 1
SOFTMAX_GAPS = 3
ROUNDS = {3: 0, 13: 1, 16: 2, 18: 3, 20: 4}
N_ROUNDS = len(ROUNDS)
SUMS_GAPS = {10: 1, 14: 2}
ROTATE_GAPS = {11: (1, 0), 12: (1, 1), 15: (2, 0), 16: (2, 1)}
POOL_STEPS, TABLES = 17, 13

USES, TAKEN_BY = [], {}
for _c, _half in ORDER[:2 * C_FF]:
    each_half = _c in (C_KV, C_VB, C_QA, C_QA + 2) or C_BB <= _c < C_BA or C_PP <= _c < C_PG
    first_half = C_KB <= _c < C_VB or _c == C_VB + 2 or C_GB <= _c < C_BB or C_BA <= _c < C_WO
    if each_half or (first_half and _half == 0):
        USES.append((_c, _half))
        TAKEN_BY[(_c, _half)] = "DVE" if C_KB <= _c < C_VB or C_BB <= _c < C_WO else "ACT"
    if 2 * (_c - GAP_CHUNK) + _half in ROUNDS:
        _r = ROUNDS[2 * (_c - GAP_CHUNK) + _half]
        USES.append(("round", _r))
        TAKEN_BY[("round", _r)] = "DVE"
TAKES = {e: [u for u in USES if TAKEN_BY[u] == e] for e in ("ACT", "DVE")}


def narrow(c):
    return c in (C_BB, C_BB + 1, C_PP, C_PP + 1)


def half_at(layer, c, half):
    return layer * (2 * CHUNKS) + (ORDER.index((c, half)) + 1 + 2 * RING)


def slot_free_at(layer, c):
    before = c - RING
    return half_at(layer, before, 1) if before >= 0 else half_at(layer, before + CHUNKS, 1) - 2 * CHUNKS


def scores_item(g):
    if g < 0 or g >= A_GAP + 2 * A_ITEMS:
        return None
    if g < A_GAP:
        return g // 2 if g % 2 == 0 else None
    return B_ITEMS + (g - A_GAP) // 2 if (g - A_GAP) % 2 == 0 else None


def transpose_item(g):
    return scores_item(g - SOFTMAX_GAPS)


def value_pair(g):
    n = transpose_item(g - 1)
    if n is None or (n < B_ITEMS and n % 2 == 0):
        return None
    return n // 2 if n < B_ITEMS else B_ITEMS // 2 + n - B_ITEMS


def build(nc, x, p, ln_emb_g, ln_emb_b, w_in, b_gate, q_norm_g, k_norm_g, w_branch_a, w_branch_b,
          w_out, ln1_g, ln1_b, w_ffn_in, w_ffn_out, ln2_g, ln2_b, w_ple_proj, w_ple_gate,
          dist_table, rope_table, identity_table, out):
    ctx = ExitStack()
    with ctx:
        def sb(name, shape, dt=F32):
            return ctx.enter_context(nc.sbuf_tensor(name, shape, dt))

        def sem(name):
            return ctx.enter_context(nc.semaphore(name))

        w_raw = sb("w_raw", [P, RING, WORDS])
        w_hi = sb("w_hi", [P, RING, WORDS], F32R)
        w_lo = sb("w_lo", [P, RING, WORDS], F32R)
        x_nat = sb("x_nat", [P, TILES, D])
        res = sb("res", [P, TILES, D])
        xT_hi = sb("xT_hi", [P, KT, SEQ], F32R)
        xT_lo = sb("xT_lo", [P, KT, SEQ], F32R)
        ln_gb = sb("ln_gb", [P, 2, D])
        dist = sb("dist", [P, TILES, B_GROUPS, SEQ])
        rope = sb("rope", [P, TILES, 2, HEAD])
        rope_q = sb("rope_q", [P, TILES, 2, HEAD])
        rope_k = sb("rope_k", [P, TILES, 2, HEAD])
        qk_gain = sb("qk_gain", [P, 2, HEAD])
        bias_raw = sb("bias_raw", [P, 2 * KT])
        bias_half = sb("bias_half", [P, 2 * KT])
        ident = sb("ident", [P, P])
        vB = sb("vB", [P, TILES, B_D])
        vA = sb("vA", [P, TILES, A_KVD])
        q_raw = sb("q_raw", [P, TILES, 512])
        q_sq = sb("q_sq", [P, TILES, 512])
        q_rot = sb("q_rot", [P, 2, TILES, 512])
        stack = sb("stack", [P, 6 * KT * P], F32R)
        o_T = sb("o_T", [P, 2, KT, SEQ], F32R)
        oBT_hi = sb("oBT_hi", [P, 2, SEQ], F32R)
        oBT_lo = sb("oBT_lo", [P, 2, SEQ], F32R)
        soft = sb("soft", [P, 3072])
        pT = sb("pT", [P, 4, SEQ], F32R)
        smax = sb("smax", [P, 4, 4])
        nbias = sb("nbias", [P, 4, 4])
        denom = sb("denom", [P, 4, 4])
        rdenom = sb("rdenom", [P, 4, 4])
        head_ms = sb("head_ms", [P, 3, 16])
        head_ve = sb("head_ve", [P, 3, 16])
        head_rstd = sb("head_rstd", [P, 3, 16])
        bn = sb("bn", [P, TILES, 2, 6])
        mean_var = sb("mean_var", [P, TILES, 2])
        ln_ve = sb("ln_ve", [P, TILES])
        ln_rstd = sb("ln_rstd", [P, TILES])
        minus_half = sb("minus_half", [P, 16])

        def heads(ap):
            return ap.rearrange("p (h s) -> p h s", s=SEQ)

        kB = stack[:, :].rearrange("p (h a s) -> p h a s", a=2, s=SEQ)
        kB_hi, kB_lo = kB[:, :, 0, :], kB[:, :, 1, :]
        qA = heads(stack[:, 0:4096])
        kA_hi, kA_lo = pT, heads(o_T[:, :, :, :].rearrange("p a k s -> p (a k s)")[:, 3072:4096])
        pT_hi, pT_lo = pT[:, 0:2, :], pT[:, 2:4, :]
        oAT_hi, oAT_lo = o_T[:, 0, :, :], o_T[:, 1, :, :]
        qB = heads(o_T[:, :, :, :].rearrange("p a k s -> p (a k s)")[:, 0:3072])
        gateB = heads(res[:, :, :].rearrange("p t d -> p (t d)"))
        gateA = heads(q_rot[:, :, :, :].rearrange("p a t n -> p (a t n)"))
        ple = q_rot[:, :, :, :].rearrange("p a t n -> p (a t n)").rearrange("p (t d) -> p t d", t=TILES)
        p_nat = vB[:, :, 0:PLE]
        act_t = q_raw
        hid = q_sq
        hT_hi, hT_lo = oAT_hi, oAT_lo

        psum = ctx.enter_context(nc.psum_tensor("psum", [P, 8, 512], F32))
        bank = [psum[:, b, :] for b in range(8)]
        acc = bank[3:7]
        ffn_bank = [(bank[0], bank[1]), (bank[2], bank[7])]
        x_bank = (bank[0], bank[1], bank[2], bank[7])

        def probs_of(n):
            if n < B_ITEMS:
                return soft[:, (n % 2) * 768:(n % 2 + 1) * 768]
            return ln_gb[:, n % 2, :]

        def probsT_of(n):
            if n < B_ITEMS:
                return soft[:, 1536 + (n % 2) * 768:1536 + (n % 2 + 1) * 768]
            return soft[:, (n % 2) * 1024:(n % 2 + 1) * 1024]

        def b_item(n):
            return 2 * (n // 4) + n % 2, (n // 2) % 2

        def b_head(h, group):
            return h * B_GROUPS + group

        def b_places(group, e):
            return slice(b_head(e, group), b_head(e + 2, group) + 1, 2 * B_GROUPS)

        def a_places(r, e):
            first = max(4 * r - 4, 0)
            return slice(first + e, first + 4, 2)

        def use_bank(use):
            return bank[USES.index(use) % 3]

        def taken(layer, use):
            takes = TAKES[TAKEN_BY[use]]
            return proj_act if TAKEN_BY[use] == "ACT" else proj_dve, layer * len(takes) + (takes.index(use) + 1)

        def ot_place(m):
            if m < B_ITEMS // 2:
                cols = slice((m % 2) * P, (m % 2 + 1) * P)
                return oBT_hi[:, m // 2, cols], oBT_lo[:, m // 2, cols], bank[7][:, m * P:(m + 1) * P]
            j = m - B_ITEMS // 2
            return oAT_hi[:, j, :], oAT_lo[:, j, :], bank[7][:, (j % 2) * SEQ:(j % 2 + 1) * SEQ]

        w_landed = [sem(f"w_landed{s}") for s in range(RING)]
        hi_split = sem("hi_split")
        lo_split = sem("lo_split")
        half_done = sem("half_done")
        x_landed = [sem(f"x_landed{t}") for t in range(TILES)]
        ident_landed = sem("ident_landed")
        rope_landed = sem("rope_landed")
        dist_landed = sem("dist_landed")
        emb_landed = sem("emb_landed")
        gb_landed = sem("gb_landed")
        small_landed = sem("small_landed")
        p_landed = sem("p_landed")
        half_set = sem("half_set")
        head_ve_set = sem("head_ve_set")
        pool_steps = sem("pool_steps")
        dve_chain = sem("dve_chain")
        var_ready = sem("var_ready")
        rstd_ready = sem("rstd_ready")
        x_ready = sem("x_ready")
        xT_done = sem("xT_done")
        xT_hi_done = sem("xT_hi_done")
        xT_lo_done = sem("xT_lo_done")
        pT_done = sem("pT_done")
        pT_hi_done = sem("pT_hi_done")
        pT_lo_done = sem("pT_lo_done")
        proj_act = sem("proj_act")
        proj_dve = sem("proj_dve")
        kqB_hi = sem("kqB_hi")
        sq_ready = sem("sq_ready")
        ms_ready = sem("ms_ready")
        head_rstd_ready = sem("head_rstd_ready")
        rotated = sem("rotated")
        qkT_done = sem("qkT_done")
        qkT_hi = sem("qkT_hi")
        scores_done = sem("scores_done")
        nbias_done = sem("nbias_done")
        exp_done = sem("exp_done")
        rdenom_done = sem("rdenom_done")
        probs_done = sem("probs_done")
        probsT_done = sem("probsT_done")
        probsT_taken = sem("probsT_taken")
        ot_done = sem("ot_done")
        ot_hi_done = sem("ot_hi_done")
        ot_lo_done = sem("ot_lo_done")
        u_done = sem("u_done")
        u_hi_done = sem("u_hi_done")
        u_lo_done = sem("u_lo_done")
        pg_tanh = sem("pg_tanh")
        pg_used = sem("pg_used")
        ff_tanh = sem("ff_tanh")
        h_done = sem("h_done")
        h_hi_done = sem("h_hi_done")
        h_lo_done = sem("h_lo_done")
        out_stored = sem("out_stored")

        def wait_alone(eng, semaphore, value):
            value = value if isinstance(value, int) else eng.to_reg(value)
            eng.wait_ge(semaphore, 1)
            eng.wait_ge(semaphore, value)

        def row_of(vector, n):
            return vector.rearrange("(a d) -> a d", a=1).broadcast_to((P, n))

        block = ctx.enter_context(nc.Block())

        @block.sync
        def _(sp):
            def rows(w, layer, k0, k, c0, n):
                return w[layer, k0 * P:(k0 + k) * P, bass.ds(c0, n)].rearrange("(k p) n -> p k n", p=P)

            def source(layer, c):
                if c < C_KB:
                    return rows(w_in, layer, 4 * (c - C_KV), 4, KA0, 512)
                if c < C_QB:
                    return rows(w_in, layer, 0, KT, KB0 + 256 * (c - C_KB), 256)
                if c < C_VB:
                    return rows(w_in, layer, 0, KT, QB0 + 256 * (c - C_QB), 256)
                if c < C_VB + 2:
                    return rows(w_in, layer, 4 * (c - C_VB), 4, VB0, 512)
                if c == C_VB + 2:
                    return rows(w_in, layer, 0, KT, VB0 + 512, 256)
                if c < C_GB:
                    return rows(w_in, layer, 4 * ((c - C_QA) % 2), 4, QA0 + 512 * ((c - C_QA) // 2), 512)
                if c < C_GA:
                    return rows(w_in, layer, 0, KT, GATE0 + D + 256 * (c - C_GB), 256)
                if c < C_BB:
                    return rows(w_in, layer, 0, KT, GATE0 + 256 * (c - C_GA), 256)
                if c < C_BA:
                    return rows(w_branch_b, layer, 0, 2, 512 * (c - C_BB), 512)
                if c < C_WO:
                    return rows(w_branch_a, layer, 0, KT, 256 * (c - C_BA), 256)
                if c < C_PP:
                    return rows(w_out, layer, 4 * ((c - C_WO) % 2), 4, 512 * ((c - C_WO) // 2), 512)
                if c < C_PG:
                    return rows(w_ple_proj, layer, 0, 2, 512 * (c - C_PP), 512)
                return rows(w_ple_gate, layer, 4 * ((c - C_PG) % 2), 4, 512 * ((c - C_PG) // 2), 512)

            def load(chunk_index, slot, src):
                k, n = src.shape[1], src.shape[2]
                wait_alone(sp, lo_split, chunk_index + 1)
                sp.dma_start(w_raw[:, slot, 0:k * n].rearrange("p (k n) -> p k n", k=k), src)\
                  .then_inc(w_landed[slot], 16)

            for t in range(TILES):
                sp.dma_start(res[:, t, :], x[0, t * P:(t + 1) * P, :]).then_inc(x_landed[t], 16)
            for c in range(AHEAD):
                load(c, c, source(0, c))
            with sp.Fori(0, DEPTH) as layer:
                for c in range(AHEAD, C_FF):
                    load(layer * CHUNKS + c, c % RING, source(layer, c))
                load(layer * CHUNKS + C_FF, C_FF % RING, rows(w_ffn_in, layer, 0, KT, 0, 256))
                load(layer * CHUNKS + (C_FF + 1), (C_FF + 1) % RING, rows(w_ffn_in, layer, 0, KT, FFN, 256))
                with sp.Fori(0, FB - 1) as f:
                    at = layer * CHUNKS + f * 3 + (C_FF + 2)
                    load(at, (C_FF + 2) % RING, rows(w_ffn_in, layer, 0, KT, f * 256 + 256, 256))
                    load(at + 1, C_FF % RING, rows(w_ffn_in, layer, 0, KT, f * 256 + (FFN + 256), 256))
                    out_rows = w_ffn_out[layer, :, :].rearrange("(b k p) n -> b p k n", k=2, p=P)
                    load(at + 2, (C_FF + 1) % RING, out_rows[f, :, :, :])
                load(layer * CHUNKS + (CHUNKS - 1), (CHUNKS - 1) % RING,
                     rows(w_ffn_out, layer, 2 * (FB - 1), 2, 0, D))
                following = (layer + 1) % DEPTH
                for c in range(AHEAD):
                    load(layer * CHUNKS + (CHUNKS + c), c, source(following, c))
            for t in range(TILES):
                sp.wait_ge(x_ready, DEPTH * 4 + t + 1)
                sp.dma_start(out[0, t * P:(t + 1) * P, :], x_nat[:, t, :]).then_inc(out_stored, 16)
            sp.wait_ge(out_stored, 16 * TILES)

        @block.gpsimd
        def _(pool):
            nc.gpsimd.memset(minus_half[:, :], -0.5).then_inc(half_set, 1)

            def ln_power(t, n, step):
                wait_alone(pool, var_ready, n)
                nc.gpsimd.tensor_scalar(ln_ve[:, t:t + 1], mean_var[:, t, 1:2], 4 * LN_EPS, None, ALU.add)\
                    .then_inc(pool_steps, 1)
                pool.wait_ge(pool_steps, step)
                nc.gpsimd.tensor_tensor(ln_rstd[:, t:t + 1], ln_ve[:, t:t + 1], minus_half[:, 0:1], ALU.pow)\
                    .then_inc(rstd_ready, 1)

            def load_gb(layer, g, b):
                pool.dma_start(ln_gb[:, 0, :], row_of(g[layer, :], D)).then_inc(gb_landed, 16)
                pool.dma_start(ln_gb[:, 1, :], row_of(b[layer, :], D)).then_inc(gb_landed, 16)

            def head_power(layer, s):
                n = 8 if s == 0 else 16
                wait_alone(pool, ms_ready, layer * 3 + (s + 1))
                nc.gpsimd.tensor_scalar(head_ve[:, s, 0:n], head_ms[:, s, 0:n], 1.0 / HEAD if s == 0 else 1.0,
                                        RMS_EPS if s == 0 else RMS_EPS / SCALE ** 2, ALU.mult, ALU.add)\
                    .then_inc(head_ve_set, 1)
                wait_alone(pool, head_ve_set, layer * 3 + (s + 1))
                nc.gpsimd.tensor_tensor(head_rstd[:, s, 0:n], head_ve[:, s, 0:n], minus_half[:, 0:n],
                                        ALU.pow).then_inc(head_rstd_ready, 1)

            def normalise(layer, n):
                wait_alone(pool, rdenom_done, layer * ITEMS + (n + 1))
                w = 768 if n < B_ITEMS else SEQ
                for i in range(1 if n < B_ITEMS else 4):
                    z = probs_of(n)[:, i * w:(i + 1) * w]
                    last = nc.gpsimd.tensor_scalar(z, z, rdenom[:, n % 4, i:i + 1], None, ALU.mult)
                last.then_inc(probs_done, 1)

            pool.wait_ge(half_set, 1)
            for t in range(TILES):
                ln_power(t, t + 1, t + 1)
            pool.dma_start(rope[:, :, :, :], rope_table).then_inc(rope_landed, 16)
            with pool.Fori(0, DEPTH) as layer:
                steps = layer * POOL_STEPS + TILES
                pool.dma_start(bias_raw[:, :], b_gate[layer, :].rearrange("(k p) -> p k", p=P),
                               allow_slow_non_contiguous=True).then_inc(small_landed, 16)
                pool.dma_start(qk_gain[:, 0, :], row_of(q_norm_g[layer, :], HEAD)).then_inc(small_landed, 16)
                pool.dma_start(qk_gain[:, 1, :], row_of(k_norm_g[layer, :], HEAD)).then_inc(small_landed, 16)
                pool.wait_ge(rope_landed, 16)
                wait_alone(pool, small_landed, layer * 48 + 48)
                nc.gpsimd.tensor_scalar(bias_half[:, :], bias_raw[:, :], 0.5, None, ALU.mult)\
                    .then_inc(pool_steps, 1)
                for part, table in ((0, rope_q), (1, rope_k)):
                    for t in range(TILES):
                        nc.gpsimd.tensor_tensor(table[:, t, 0, :], rope[:, t, 0, :], qk_gain[:, part, :],
                                                ALU.mult).then_inc(pool_steps, 1)
                        for half in range(2):
                            def halves(ap, h):
                                return ap.rearrange("p (a h j) -> p a h j", a=2, h=2)[:, :, h, :]
                            nc.gpsimd.tensor_tensor(halves(table[:, t, 1, :], half),
                                                    halves(rope[:, t, 1, :], half),
                                                    halves(qk_gain[:, part, :], 1 - half),
                                                    ALU.mult).then_inc(pool_steps, 1)
                wait_alone(pool, pool_steps, steps + TABLES)
                head_power(layer, 0)
                for n in range(ITEMS):
                    normalise(layer, n)
                    if n == 5:
                        head_power(layer, 1)
                    if n == B_ITEMS:
                        head_power(layer, 2)
                    if n == B_ITEMS + 1:
                        wait_alone(pool, ot_done, layer * VALUES + B_ITEMS // 2)
                        pool.dma_start(p_nat, p[layer, 0, :, :].rearrange("(t p) d -> p t d", p=P))\
                            .then_inc(p_landed, 16)
                wait_alone(pool, probsT_done, layer * ITEMS + ITEMS)
                load_gb(layer, ln1_g, ln1_b)
                for t in range(TILES):
                    ln_power(t, layer * 4 + (TILES + t + 1), steps + (TABLES + t + 1))
                wait_alone(pool, x_ready, layer * 4 + 4)
                load_gb(layer, ln2_g, ln2_b)
                for t in range(TILES):
                    ln_power(t, layer * 4 + (2 * TILES + t + 1), steps + (TABLES + TILES + t + 1))

        @block.scalar
        def _(act):
            def split_hi(free, landed, slot, words=WORDS):
                act.wait_ge(w_landed[slot], landed)
                act.wait_ge(half_done, free)
                nc.scalar.activation(w_hi[:, slot, 0:words], w_raw[:, slot, 0:words], ACT.Copy)\
                    .then_inc(hi_split, 1)

            def x_transposes(n, t):
                for half in range(2):
                    act.wait_ge(xT_done, n + (2 * t + half + 1))
                    nc.scalar.activation(xT_hi[:, 4 * half:4 * half + 4, t * P:(t + 1) * P],
                                         x_bank[2 * t + half].rearrange("p (k s) -> p k s", k=4), ACT.Copy)\
                        .then_inc(xT_hi_done, 1)

            def take(layer, c, half, dst, src, last=True):
                act.wait_ge(half_done, half_at(layer, c, half))
                i = nc.scalar.activation(dst, src, ACT.Copy)
                if last:
                    i.then_inc(proj_act, 1)

            def slab(layer, s):
                w = 256 if s == 0 else 512
                c = C_KV + 1 if s == 0 else C_QA - 1 + 2 * s
                if s:
                    act.wait_ge(rotated, layer * 3 + s)
                for t in range(TILES):
                    src = use_bank((c - 1, t))
                    if s == 0:
                        take(layer, c, t, q_raw[:, t, 0:256], src[:, 0:256], last=False)
                        take(layer, c, t, vA[:, t, :], src[:, 256:512])
                    else:
                        take(layer, c, t, q_raw[:, t, :], src)
                act.wait_ge(*taken(layer, (c - 1, 1)))
                nc.scalar.activation(q_sq[:, :, 0:w], q_raw[:, :, 0:w], ACT.Square).then_inc(sq_ready, 1)

            def upper_parts(src, e, dst, own, twice):
                rows = slice(HEAD * e, HEAD * e + HEAD)
                for half in range(2) if twice else (e,):
                    i = nc.scalar.activation(dst[HEAD * half:HEAD * half + HEAD, own, :], src[rows, :, :], ACT.Copy)
                return i

            def mixer_b_hi(layer, c):
                act.wait_ge(half_done, half_at(layer, c, 1))
                for e in range(2):
                    i = upper_parts(heads(use_bank((c, 0))), e, kB_hi if c < C_QB else qB, b_places((c - C_KB) % 3, e),
                                    c < C_QB)
                i.then_inc(kqB_hi, 1)

            def gap(layer, g):
                if g in ROUNDS:
                    r = ROUNDS[g]
                    act.wait_ge(qkT_done, layer * N_ROUNDS + (r + 1))
                    for e in range(2):
                        i = upper_parts(heads(use_bank(("round", r))), e, kA_hi if r == 0 else qA, a_places(r, e), r == 0)
                    i.then_inc(qkT_hi, 1)
                n = transpose_item(g)
                if n is not None:
                    act.wait_ge(probsT_done, layer * ITEMS + (n + 1))
                    if 2 <= n < B_ITEMS:
                        act.wait_ge(ot_done, layer * VALUES + n // 2)
                    elif n > B_ITEMS:
                        act.wait_ge(ot_done, layer * VALUES + (B_ITEMS // 2 + n - B_ITEMS - 1))
                    src = psum[:, 5:7, :].rearrange("p b n -> p (b n)")
                    w = 768 if n < B_ITEMS else 1024
                    nc.scalar.activation(probsT_of(n), src[:, 0:w], ACT.Copy).then_inc(probsT_taken, 1)
                m = value_pair(g)
                if m is not None:
                    act.wait_ge(ot_done, layer * VALUES + (m + 1))
                    hi, _, src = ot_place(m)
                    nc.scalar.activation(hi, src, ACT.Copy).then_inc(ot_hi_done, 1)
                n = scores_item(g)
                if n is not None:
                    act.wait_ge(nbias_done, layer * ITEMS + (n + 1))
                    z = probs_of(n)
                    if n < B_ITEMS:
                        e = nc.scalar.activation(z, z, ACT.Exp, bias=nbias[:, n % 4, 0:1], scale=SCALE,
                                                 accum_out=denom[:, n % 4, 0:1])
                    else:
                        for i in range(4):
                            head, t = 2 * (n - B_ITEMS) + i // 2, i % 2
                            at = t * 8 + head % 8
                            e = nc.scalar.activation(z[:, i * SEQ:(i + 1) * SEQ],
                                                     bank[3 + i // 2][:, t * SEQ:(t + 1) * SEQ], ACT.Exp,
                                                     bias=nbias[:, n % 4, i:i + 1],
                                                     scale=head_rstd[:, 1 + head // 8, at:at + 1],
                                                     accum_out=denom[:, n % 4, i:i + 1])
                    e.then_inc(exp_done, 1)

            act.dma_start(ident[:, :], identity_table).then_inc(ident_landed, 16)
            act.dma_start(ln_gb[:, 0, :], row_of(ln_emb_g, D)).then_inc(emb_landed, 16)
            act.dma_start(ln_gb[:, 1, :], row_of(ln_emb_b, D)).then_inc(emb_landed, 16)
            act.dma_start(dist[:, :, :, :], dist_table).then_inc(dist_landed, 16)
            for c in range(AHEAD):
                split_hi(slot_free_at(0, c), 16, c)
            x_transposes(0, 0)
            with act.Fori(0, DEPTH) as layer:
                x_transposes(layer * 8, 1)

                def ahead(c):
                    split_hi(slot_free_at(layer, c + AHEAD), layer * (16 * CHUNKS // RING)
                             + 16 * ((c + AHEAD) // RING + 1), (c + AHEAD) % RING,
                             WORDS // 2 if narrow(c + AHEAD) else WORDS)

                def ple_tanh(h, t):
                    n = 2 * h + t
                    act.wait_ge(half_done, half_at(layer, C_PG + 2 * h + 1, t))
                    if n >= 2:
                        act.wait_ge(pg_used, layer * 4 + (n - 1))
                    nc.scalar.activation(act_t[:, n % 2, :], acc[2 * t + h], ACT.Tanh, scale=0.5)\
                        .then_inc(pg_tanh, 1)

                for c in range(C_FF):
                    if c == C_PG + 1:
                        ple_tanh(0, 0)
                    ahead(c)
                    if C_KB <= c < C_VB:
                        mixer_b_hi(layer, c)
                    for half in range(2):
                        if c == C_VB + 1:
                            take(layer, c, half, vB[:, half, 0:512], use_bank((C_VB, half)))
                        if c == C_VB + 2 and half == 1:
                            take(layer, c, 1, vB[:, :, 512:768],
                                 use_bank((c, 0)).rearrange("p (t n) -> p t n", t=TILES))
                        if half == 1 and c in (C_KV + 1, C_QA + 1, C_QA + 3):
                            slab(layer, {C_KV + 1: 0, C_QA + 1: 1, C_QA + 3: 2}[c])
                        if half == 1 and C_GB <= c < C_BB:
                            q = (c - C_GB) % 4
                            dst, b0 = (gateB, KT) if c < C_GA else (gateA, 0)
                            act.wait_ge(half_done, half_at(layer, c, 1))
                            src = heads(use_bank((c, 0)))
                            for b in range(2):
                                i = nc.scalar.activation(dst[:, 2 * q + b, :], src[:, b, :],
                                                         ACT.Tanh, scale=0.5,
                                                         bias=bias_half[:, b0 + 2 * q + b:b0 + 2 * q + b + 1])
                            i.then_inc(proj_act, 1)
                        if GAP_CHUNK <= c < C_BA:
                            gap(layer, 2 * (c - GAP_CHUNK) + half)
                    if C_BA <= c < C_WO:
                        q = c - C_BA
                        act.wait_ge(u_done, layer * 4 + (q + 1))
                        nc.scalar.activation(xT_hi[:, 2 * q:2 * q + 2, :], gateA[:, 2 * q:2 * q + 2, :],
                                             ACT.Copy).then_inc(u_hi_done, 1)
                    if c == C_WO:
                        act.wait_ge(pT_done, layer + 1)
                        nc.scalar.activation(pT_hi[:, :, :], heads(bank[7]), ACT.Copy).then_inc(pT_hi_done, 1)
                    if C_PP <= c < C_PG:
                        for t in range(TILES):
                            take(layer, c, t, ple[:, t, (c - C_PP) * 512:(c - C_PP + 1) * 512], use_bank((c, t)))
                    if c == C_PG - 1:
                        for t in range(TILES):
                            x_transposes(layer * 8 + 4, t)
                    if c == C_PG + 1:
                        ple_tanh(0, 1)
                    if c == C_PG + 3:
                        for t in range(TILES):
                            ple_tanh(1, t)

                def ffn_tanh(gate_chunk, b):
                    act.wait_ge(half_done, layer * (2 * CHUNKS) + gate_chunk * 2 + (2 + 2 * RING))
                    nc.scalar.activation(act_t[:, b, :], ffn_bank[b][0], ACT.Tanh, scale=0.5)\
                        .then_inc(ff_tanh, 1)

                def hidden_hi(fi, b):
                    act.wait_ge(h_done, layer * FB + fi + 1)
                    nc.scalar.activation(hT_hi[:, 2 * b:2 * b + 2, :], heads(hid[:, b, :]), ACT.Copy)\
                        .then_inc(h_hi_done, 1)

                def ahead_ffn(fi, j, slot):
                    split_hi(layer * (2 * CHUNKS) + fi * 6 + (2 * (C_FF + 2 + j) + 2 * RING),
                             layer * (16 * CHUNKS // RING) + fi * 16 + 16 * ((C_FF + 4 + j) // RING + 1), slot)

                ahead(C_FF)
                ahead(C_FF + 1)
                act.wait_ge(pg_used, layer * 4 + 4)
                ffn_tanh(C_FF, 0)
                hidden_hi(0, 0)
                with act.Fori(0, (FB - 1) // 2) as pair:
                    for b in range(2):
                        f = pair * 2 + b
                        ahead_ffn(f, 0, (C_FF + 4) % RING)
                        ahead_ffn(f, 1, (C_FF + 5) % RING)
                        ffn_tanh(f * 3 + (C_FF + 2), 1 - b)
                        hidden_hi(f + 1, 1 - b)
                        ahead_ffn(f, 2, (C_FF + 6) % RING)
                ahead(CHUNKS - 1)
                x_transposes(layer * 8 + 8, 0)

        @block.vector
        def _(dve):
            DC = 400
            used = [0]
            base = [0]

            def link(ins):
                used[0] += 1
                ins.then_inc(dve_chain, 1)
                dve.wait_ge(dve_chain, base[0] + used[0])

            def split_lo(index, slot, words=WORDS):
                dve.wait_ge(hi_split, index + 1)
                nc.vector.tensor_tensor(w_lo[:, slot, 0:words], w_raw[:, slot, 0:words],
                                        w_hi[:, slot, 0:words].bitcast(F32),
                                        ALU.subtract).then_inc(lo_split, 1)

            def statistics(t, half):
                i = nc.vector.bn_stats(bn[:, t, half, :], res[:, t, half * 512:half * 512 + 512])
                if half == 1:
                    used[0] += 1
                    i.then_inc(dve_chain, 1)

            def layer_norm(t, n, gains, landed):
                wait_alone(dve, dve_chain, base[0] + used[0])
                nc.vector.bn_aggr(mean_var[:, t, :], bn[:, t, :, :]).then_inc(var_ready, 1)
                dve.wait_ge(gains, landed)
                dve.wait_ge(var_ready, n + 1)
                link(nc.vector.scalar_tensor_tensor(x_nat[:, t, :], res[:, t, :], mean_var[:, t, 0:1],
                                                    ln_gb[:, 0, :], ALU.subtract, ALU.mult))
                dve.wait_ge(rstd_ready, n + 1)
                nc.vector.scalar_tensor_tensor(x_nat[:, t, :], x_nat[:, t, :], ln_rstd[:, t:t + 1],
                                               ln_gb[:, 1, :], ALU.mult, ALU.add).then_inc(x_ready, 1)

            def x_transposes(n, t):
                for half in range(2):
                    dve.wait_ge(xT_hi_done, n + (2 * t + half + 1))
                    at = (slice(None), slice(4 * half, 4 * half + 4), slice(t * P, (t + 1) * P))
                    nc.vector.tensor_tensor(xT_lo[at], x_bank[2 * t + half].rearrange("p (k s) -> p k s", k=4),
                                            xT_hi[at].bitcast(F32), ALU.subtract).then_inc(xT_lo_done, 1)

            def lower_parts(src, e, hi, lo, own, twice):
                rows = slice(HEAD * e, HEAD * e + HEAD)
                for half in range(2) if twice else (1 - e,):
                    i = nc.vector.tensor_tensor(lo[HEAD * half:HEAD * half + HEAD, own, :], src[rows, :, :],
                                                hi[rows, own, :].bitcast(F32), ALU.subtract)
                return i

            def mixer_b_lo(layer, c):
                dve.wait_ge(kqB_hi, layer * 6 + (c - C_KB + 1))
                for e in range(2):
                    i = lower_parts(heads(use_bank((c, 0))), e, *((kB_hi, kB_lo) if c < C_QB else (qB, qB)),
                                    b_places((c - C_KB) % 3, e), c < C_QB)
                i.then_inc(proj_dve, 1)

            def slab_views(s):
                w = 256 if s == 0 else 512
                return w // HEAD, [a[:, :, 0:w].rearrange("p t (h d) -> p t h d", d=HEAD) for a in (q_raw, q_sq)]

            def sums(layer, s):
                nh, (_, sq) = slab_views(s)
                dve.wait_ge(sq_ready, layer * 3 + (s + 1))
                nc.vector.tensor_reduce(head_ms[:, s, 0:2 * nh].rearrange("p (t h) -> p t h", t=TILES), sq,
                                        AX_X, ALU.add).then_inc(ms_ready, 1)

            def rotate(layer, s, t):
                nh, (raw, sq) = slab_views(s)
                table = rope_k if s == 0 else rope_q
                if t == 0:
                    dve.wait_ge(ms_ready, layer * 3 + (s + 1))
                if s == 0 and t == 0:
                    dve.wait_ge(pool_steps, layer * POOL_STEPS + (TABLES + TILES))
                    dve.wait_ge(head_rstd_ready, layer * 3 + 1)
                    rs = head_rstd[:, 0, 0:2 * nh].rearrange("p (t h) -> p t h", t=TILES).unsqueeze(3)\
                        .broadcast_to((P, TILES, nh, HEAD))
                    link(nc.vector.tensor_tensor(raw, raw, rs, ALU.mult))

                def part(ap, h):
                    return ap.rearrange("p h (a b j) -> p h a b j", a=2, b=2)[:, :, :, h, :]
                for half in range(2):
                    sine = table[:, t, 1, :].rearrange("p (a b j) -> p a b j", a=2, b=2)[:, :, half, :]\
                        .unsqueeze(1).broadcast_to((P, nh, 2, 16))
                    i = nc.vector.tensor_tensor(part(sq[:, t, :, :], half), part(raw[:, t, :, :], 1 - half),
                                                sine, ALU.mult)
                link(i)
                cosine = table[:, t, 0, :].unsqueeze(1).broadcast_to((P, nh, HEAD))
                link(nc.vector.tensor_tensor(raw[:, t, :, :], raw[:, t, :, :], cosine, ALU.mult))
                if s == 2 and t == 0:
                    dve.wait_ge(qkT_done, layer * N_ROUNDS + 1)
                w = nh * HEAD
                i = nc.vector.tensor_tensor(q_rot[:, s % 2, t, 0:w], q_raw[:, t, 0:w], q_sq[:, t, 0:w], ALU.add)
                if t == 1:
                    i.then_inc(rotated, 1)

            def maxima(layer, n):
                dve.wait_ge(scores_done, layer * ITEMS + (n + 1))
                if n < B_ITEMS:
                    h, t = b_item(n)
                    if n == 0:
                        dve.wait_ge(dist_landed, 16)
                    if n >= 2:
                        dve.wait_ge(probsT_done, layer * ITEMS + (n - 1))
                    z = probs_of(n)
                    for gr in range(B_GROUPS):
                        i = nc.vector.scalar_tensor_tensor(
                            z[:, gr * SEQ:(gr + 1) * SEQ], dist[:, t, gr, :],
                            SLOPE[gr * B_PER_GROUP + h] / SCALE,
                            bank[3 + gr // 2][:, (gr % 2) * SEQ:(gr % 2 + 1) * SEQ], ALU.mult, ALU.add)
                    link(i)
                    link(nc.vector.reduce_max(smax[:, n % 4, 0:1], z, AX_X))
                    nc.vector.tensor_scalar(nbias[:, n % 4, 0:1], smax[:, n % 4, 0:1], -SCALE, None,
                                            ALU.mult).then_inc(nbias_done, 1)
                else:
                    j = n - B_ITEMS
                    if j >= 2:
                        dve.wait_ge(probsT_done, layer * ITEMS + (n - 1))
                    if j % 4 == 0:
                        dve.wait_ge(head_rstd_ready, layer * 3 + (2 + j // 4))
                    link(nc.vector.reduce_max(smax[:, n % 4, :], psum[:, 3:5, :].rearrange("p b n -> p (b n)")
                                              .rearrange("p (i s) -> p i s", s=SEQ), AX_X))
                    at = (2 * j) % 8
                    scale = head_rstd[:, 1 + j // 4, :].rearrange("p (t h) -> p h t", t=TILES)[:, at:at + 2, :]
                    pairs = [a[:, n % 4, :].rearrange("p (h t) -> p h t", h=2) for a in (nbias, smax)]
                    nc.vector.scalar_tensor_tensor(pairs[0], pairs[1], -1.0, scale, ALU.mult, ALU.mult)\
                        .then_inc(nbias_done, 1)

            def gap(layer, g):
                n = scores_item(g)
                if n is not None:
                    maxima(layer, n)
                n = scores_item(g - 1)
                if n is not None:
                    k = 1 if n < B_ITEMS else 4
                    dve.wait_ge(exp_done, layer * ITEMS + (n + 1))
                    nc.vector.reciprocal(rdenom[:, n % 4, 0:k], denom[:, n % 4, 0:k]).then_inc(rdenom_done, 1)
                if g in ROUNDS:
                    r = ROUNDS[g]
                    dve.wait_ge(qkT_hi, layer * N_ROUNDS + (r + 1))
                    for e in range(2):
                        i = lower_parts(heads(use_bank(("round", r))), e,
                                        *((kA_hi, kA_lo) if r == 0 else (qA, qA)), a_places(r, e), r == 0)
                    i.then_inc(proj_dve, 1)
                m = value_pair(g)
                if m is not None:
                    hi, lo, src = ot_place(m)
                    dve.wait_ge(ot_hi_done, layer * VALUES + (m + 1))
                    nc.vector.tensor_tensor(lo, src, hi.bitcast(F32), ALU.subtract).then_inc(ot_lo_done, 1)
                if g in SUMS_GAPS:
                    sums(layer, SUMS_GAPS[g])
                if g in ROTATE_GAPS:
                    rotate(layer, *ROTATE_GAPS[g])

            dve.sem_inc(lo_split, RING)
            for t in range(TILES):
                dve.wait_ge(x_landed[t], 16)
                link(nc.vector.tensor_scalar(res[:, t, :], res[:, t, :], 2.0, None, ALU.mult))
                for half in range(2):
                    statistics(t, half)
                layer_norm(t, t, emb_landed, 32)
            x_transposes(0, 0)
            for c in range(AHEAD):
                split_lo(c, c)
            start = used[0]
            with dve.Fori(0, DEPTH) as layer:
                used[0] = 0
                base[0] = layer * DC + start
                x_transposes(layer * 8, 1)

                def ahead(c):
                    split_lo(layer * CHUNKS + (c + AHEAD), (c + AHEAD) % RING,
                             WORDS // 2 if narrow(c + AHEAD) else WORDS)

                def residual(h, t):
                    cols = slice(h * 512, (h + 1) * 512)
                    dve.wait_ge(half_done, half_at(layer, C_WO + 2 * h + 1, t))
                    link(nc.vector.scalar_tensor_tensor(res[:, t, cols], x_nat[:, t, cols], 2 * ALPHA,
                                                        acc[2 * t + h], ALU.mult, ALU.add))
                    statistics(t, h)

                def ple_add(h, t):
                    n = 2 * h + t
                    cols = slice(h * 512, (h + 1) * 512)
                    dve.wait_ge(pg_tanh, layer * 4 + (n + 1))
                    if n == 0:
                        dve.wait_ge(*taken(layer, (C_PG - 1, 1)))
                    if n < 2:
                        dve.wait_ge(x_ready, layer * 4 + (TILES + t + 1))
                    nc.vector.scalar_tensor_tensor(ple[:, t, cols], act_t[:, n % 2, :], 1.0,
                                                   ple[:, t, cols], ALU.add, ALU.mult).then_inc(pg_used, 1)
                    dve.wait_ge(pg_used, layer * 4 + (n + 1))
                    link(nc.vector.scalar_tensor_tensor(res[:, t, cols], x_nat[:, t, cols], 2 * ALPHA,
                                                        ple[:, t, cols], ALU.mult, ALU.add))

                for c in range(C_FF):
                    if c == C_WO + 3:
                        residual(1, 0)
                        layer_norm(0, layer * 4 + TILES, gb_landed, layer * 64 + 32)
                    if c == C_PG + 1:
                        ple_add(0, 0)
                    ahead(c)
                    if C_KB <= c < C_VB:
                        mixer_b_lo(layer, c)
                    if c == C_KB:
                        sums(layer, 0)
                    if c == C_QB:
                        for t in range(TILES):
                            rotate(layer, 0, t)
                    for half in range(2):
                        if GAP_CHUNK <= c < C_BA:
                            gap(layer, 2 * (c - GAP_CHUNK) + half)
                        if C_BB <= c < C_BA:
                            q = 2 * (c - C_BB) + half
                            if q == 0:
                                dve.wait_ge(*taken(layer, (C_BB - 1, 0)))
                            dve.wait_ge(half_done, half_at(layer, c, half))
                            nc.vector.scalar_tensor_tensor(gateB[:, 2 * q:2 * q + 2, :], gateB[:, 2 * q:2 * q + 2, :],
                                                           1.0, heads(use_bank((c, half))), ALU.add, ALU.mult)\
                                .then_inc(proj_dve, 1)
                    if C_BA <= c < C_WO:
                        q = c - C_BA
                        ga = gateA[:, 2 * q:2 * q + 2, :]
                        dve.wait_ge(half_done, half_at(layer, c, 1))
                        nc.vector.scalar_tensor_tensor(ga, ga, 1.0, heads(use_bank((c, 0))), ALU.add, ALU.mult)\
                            .then_inc(proj_dve, 1)
                        dve.wait_ge(*taken(layer, (c, 0)))
                        nc.vector.tensor_tensor(ga, ga, gateB[:, 2 * q:2 * q + 2, :], ALU.add).then_inc(u_done, 1)
                        dve.wait_ge(u_hi_done, layer * 4 + (q + 1))
                        nc.vector.tensor_tensor(xT_lo[:, 2 * q:2 * q + 2, :], ga,
                                                xT_hi[:, 2 * q:2 * q + 2, :].bitcast(F32), ALU.subtract)\
                            .then_inc(u_lo_done, 1)
                    if c == C_WO:
                        dve.wait_ge(pT_hi_done, layer + 1)
                        nc.vector.tensor_tensor(pT_lo[:, :, :], heads(bank[7]), pT_hi[:, :, :].bitcast(F32),
                                                ALU.subtract).then_inc(pT_lo_done, 1)
                    if c == C_WO + 1:
                        for t in range(TILES):
                            residual(0, t)
                    if c == C_WO + 3:
                        residual(1, 1)
                        layer_norm(1, layer * 4 + (TILES + 1), gb_landed, layer * 64 + 32)
                    if c == C_PG - 1:
                        for t in range(TILES):
                            x_transposes(layer * 8 + 4, t)
                    if c == C_PG + 1:
                        ple_add(0, 1)
                    if c == C_PG + 3:
                        for t in range(TILES):
                            ple_add(1, t)

                def hidden(fi, up_chunk, b):
                    dve.wait_ge(ff_tanh, layer * FB + fi + 1)
                    dve.wait_ge(half_done, layer * (2 * CHUNKS) + up_chunk * 2 + (2 + 2 * RING))
                    link(nc.vector.scalar_tensor_tensor(hid[:, b, :], act_t[:, b, :], 1.0, ffn_bank[b][0],
                                                        ALU.add, ALU.mult))
                    nc.vector.tensor_tensor(hid[:, b, :], hid[:, b, :], ffn_bank[b][1], ALU.mult)\
                        .then_inc(h_done, 1)

                def hidden_lo(fi, b):
                    dve.wait_ge(h_hi_done, layer * FB + fi + 1)
                    nc.vector.tensor_tensor(hT_lo[:, 2 * b:2 * b + 2, :], heads(hid[:, b, :]),
                                            hT_hi[:, 2 * b:2 * b + 2, :].bitcast(F32), ALU.subtract)\
                        .then_inc(h_lo_done, 1)

                ahead(C_FF)
                ahead(C_FF + 1)
                hidden(0, C_FF + 1, 0)
                hidden_lo(0, 0)
                before = used[0]
                with dve.Fori(0, (FB - 1) // 2) as pair:
                    base[0] = layer * DC + pair * 2 + start
                    for b in range(2):
                        f = pair * 2 + b
                        at = layer * CHUNKS + f * 3 + (C_FF + 4)
                        split_lo(at, (C_FF + 4) % RING)
                        split_lo(at + 1, (C_FF + 5) % RING)
                        hidden(f + 1, f * 3 + (C_FF + 3), 1 - b)
                        hidden_lo(f + 1, 1 - b)
                        split_lo(at + 2, (C_FF + 6) % RING)
                assert used[0] == before + 2
                used[0] = before + FB - 1
                base[0] = layer * DC + start

                def last_residual(t):
                    dve.wait_ge(half_done, half_at(layer, CHUNKS - 1, t))
                    for h in range(2):
                        cols = slice(h * 512, (h + 1) * 512)
                        link(nc.vector.tensor_tensor(res[:, t, cols], res[:, t, cols], acc[2 * t + h], ALU.add))
                        statistics(t, h)

                last_residual(0)
                layer_norm(0, layer * 4 + 2 * TILES, gb_landed, layer * 64 + 64)
                last_residual(1)
                x_transposes(layer * 8 + 8, 0)
                ahead(CHUNKS - 1)
                layer_norm(1, layer * 4 + (2 * TILES + 1), gb_landed, layer * 64 + 64)
                assert used[0] < DC
                dve.sem_inc(dve_chain, DC - used[0])

        @block.tensor
        def _(pe):
            def product(dst, l_hi, l_lo, r_hi, r_lo, start, stop):
                nc.tensor.matmul(dst, l_hi, r_hi, start=start, stop=False)
                nc.tensor.matmul(dst, l_hi, r_lo, start=False, stop=False)
                return nc.tensor.matmul(dst, l_lo, r_hi, start=False, stop=stop)

            def weights(layer, c):
                pe.wait_ge(lo_split, layer * CHUNKS + (c + 1 + RING))

            def chunk(slot, k, n):
                return [w[:, slot, 0:k * n].rearrange("p (k n) -> p k n", k=k) for w in (w_hi, w_lo)]

            def stationary(slot, k, n, block_, dst, r_hi, r_lo, before_last=None):
                hi, lo = chunk(slot, k, n)
                cols = slice(block_ * P, (block_ + 1) * P)
                for kt in range(k):
                    if kt == k - 1 and before_last is not None:
                        pe.wait_ge(*before_last)
                    i = product(dst, hi[:, kt, cols], lo[:, kt, cols], r_hi[:, kt, :], r_lo[:, kt, :],
                                kt == 0, kt == k - 1)
                return i

            def moving(slot, k, n, cols, dst, l_hi, l_lo, k0, t, start, stop):
                hi, lo = chunk(slot, k, n)
                rows = slice(t * P, (t + 1) * P)
                for kt in range(k):
                    i = product(dst, l_hi[:, k0 + kt, rows], l_lo[:, k0 + kt, rows], hi[:, kt, cols],
                                lo[:, kt, cols], start and kt == 0, stop and kt == k - 1)
                return i

            def bank_free(layer, use):
                at = USES.index(use)
                if at >= 3:
                    pe.wait_ge(*taken(layer, USES[at - 3]))

            def x_transposes(n, t):
                pe.wait_ge(x_ready, n + 1)
                for half in range(2):
                    for k in range(4):
                        kt = 4 * half + k
                        i = nc.tensor.transpose(x_bank[2 * t + half][:, k * P:(k + 1) * P],
                                                x_nat[:, t, kt * P:(kt + 1) * P], ident[:, :])
                    i.then_inc(xT_done, 1)

            def qk_round(layer, r):
                bank_free(layer, ("round", r))
                slab = 0 if r == 0 else 1 + (r - 1) // 2
                pe.wait_ge(rotated, layer * 3 + (slab + 1))
                for b in range(2):
                    first = P * b + (0 if r == 0 else 2 * P * ((r - 1) % 2))
                    for t in range(TILES):
                        at = b * SEQ + t * P
                        i = nc.tensor.transpose(use_bank(("round", r))[:, at:at + P],
                                                q_rot[:, slab % 2, t, first:first + P], ident[:, :])
                i.then_inc(qkT_done, 1)

            def scores(layer, n):
                if n == 0:
                    pe.wait_ge(*taken(layer, (C_VB - 1, 0)))
                elif n <= B_ITEMS:
                    pe.wait_ge(nbias_done, layer * ITEMS + n)
                else:
                    pe.wait_ge(exp_done, layer * ITEMS + n)
                if n < B_ITEMS:
                    h, t = b_item(n)
                    for gr in range(B_GROUPS):
                        dst = bank[3 + gr // 2][:, (gr % 2) * SEQ:(gr % 2 + 1) * SEQ]
                        own = b_head(h, gr)
                        nc.tensor.matmul(dst, qB[:, own, t * P:(t + 1) * P], kB_hi[:, own, :], start=True, stop=False)
                        i = nc.tensor.matmul(dst, qB[:, own, t * P:(t + 1) * P], kB_lo[:, own, :],
                                             start=False, stop=True)
                else:
                    j = n - B_ITEMS
                    if j % 2 == 0:
                        pe.wait_ge(*taken(layer, ("round", j // 2 + 1)))
                    for e in range(2):
                        for t in range(TILES):
                            dst = bank[3 + e][:, t * SEQ:(t + 1) * SEQ]
                            q = qA[:, 2 * j + e, t * P:(t + 1) * P]
                            nc.tensor.matmul(dst, q, kA_hi[:, j // 2, :], start=True, stop=False)
                            i = nc.tensor.matmul(dst, q, kA_lo[:, j // 2, :], start=False, stop=True)
                i.then_inc(scores_done, 1)

            def transposes(layer, n):
                pe.wait_ge(probs_done, layer * ITEMS + (n + 1))
                if n > 0:
                    pe.wait_ge(probsT_taken, layer * ITEMS + n)
                z = probs_of(n)
                flat = psum[:, 5:7, :].rearrange("p b n -> p (b n)")
                if n < B_ITEMS:
                    for at in range(0, 768, P):
                        i = nc.tensor.transpose(flat[:, at:at + P], z[:, at:at + P], ident[:, :])
                else:
                    for e in range(2):
                        for kt in range(2):
                            for t in range(TILES):
                                at = e * 512 + t * SEQ + kt * P
                                to = e * 512 + kt * SEQ + t * P
                                i = nc.tensor.transpose(flat[:, to:to + P], z[:, at:at + P], ident[:, :])
                i.then_inc(probsT_done, 1)

            def values(layer, m):
                _, _, dst = ot_place(m)
                if m > 0:
                    pe.wait_ge(ot_lo_done, layer * VALUES + m)
                if m < B_ITEMS // 2:
                    n = 2 * m + 1
                    pe.wait_ge(probsT_taken, layer * ITEMS + (n + 1))
                    if m == 0:
                        pe.wait_ge(*taken(layer, (C_VB + 2, 0)))
                    for step in range(6):
                        gr, kt = step // 2, step % 2
                        for e in range(2):
                            own = gr * B_PER_GROUP + b_item(n - 1 + e)[0]
                            i = nc.tensor.matmul(dst[HEAD * e:HEAD * e + HEAD, :],
                                                 vB[:, kt, own * HEAD:(own + 1) * HEAD],
                                                 probsT_of(n - 1 + e)[:, step * P:(step + 1) * P],
                                                 start=step == 0, stop=step == 5)
                else:
                    j = m - B_ITEMS // 2
                    pe.wait_ge(probsT_taken, layer * ITEMS + (B_ITEMS + j + 1))
                    for kt in range(2):
                        for e in range(2):
                            i = nc.tensor.matmul(dst[HEAD * e:HEAD * e + HEAD, :],
                                                 vA[:, kt, (j // 2) * HEAD:(j // 2 + 1) * HEAD],
                                                 probsT_of(B_ITEMS + j)[:, e * 512 + kt * SEQ:e * 512 + (kt + 1) * SEQ],
                                                 start=kt == 0, stop=kt == 1)
                i.then_inc(ot_done, 1)

            def gap(layer, g):
                n = scores_item(g)
                if n is not None:
                    scores(layer, n)
                if g in ROUNDS:
                    qk_round(layer, ROUNDS[g])
                n = transpose_item(g)
                if n is not None:
                    transposes(layer, n)
                m = value_pair(g)
                if m is not None:
                    values(layer, m)

            pe.sem_inc(half_done, 2 * RING)
            pe.wait_ge(ident_landed, 16)
            x_transposes(0, 0)
            with pe.Fori(0, DEPTH) as layer:
                def use_half(c, half):
                    s = c % RING
                    if half == 0:
                        weights(layer, c)
                    opened = (c, half) if (c, half) in USES else (c, 0) if (c, 0) in USES else (c - 1, half)
                    if (c, half) in USES:
                        bank_free(layer, opened)
                    if C_KB <= c < C_VB or C_GB <= c < C_BB or C_BA <= c < C_WO:
                        r = (oAT_hi, oAT_lo) if c >= C_BA else (xT_hi, xT_lo)
                        late = (ot_lo_done, layer * VALUES + VALUES) if (c, half) == (C_BA, 0) else None
                        return stationary(s, KT, 256, half, use_bank(opened)[:, half * SEQ:(half + 1) * SEQ], *r,
                                          before_last=late)
                    if C_BB <= c < C_BA:
                        for b in range(2):
                            i = stationary(s, 2, 512, 2 * half + b, use_bank(opened)[:, b * SEQ:(b + 1) * SEQ],
                                           oBT_hi, oBT_lo)
                        return i
                    if c == C_VB + 2:
                        return moving(s, KT, 256, slice(0, 256), use_bank(opened)[:, half * SEQ:(half + 1) * SEQ],
                                      xT_hi, xT_lo, 0, half, True, True)
                    if c < C_GB:
                        first = c in (C_KV, C_VB, C_QA, C_QA + 2)
                        return moving(s, 4, 512, slice(0, 512), use_bank(opened), xT_hi, xT_lo,
                                      0 if first else 4, half, first, not first)
                    if C_PP <= c < C_PG:
                        return moving(s, 2, 512, slice(0, 512), use_bank(opened), pT_hi, pT_lo, 0, half, True, True)
                    k, h = ((c - C_WO) if c < C_PP else (c - C_PG)) % 2, \
                        ((c - C_WO) if c < C_PP else (c - C_PG)) // 2
                    return moving(s, 4, 512, slice(0, 512), acc[2 * half + h], xT_hi, xT_lo, 4 * k, half,
                                  k == 0, k == 1)

                def ffn_in(slot, b, part):
                    for half in range(2):
                        i = stationary(slot, KT, 256, half, ffn_bank[b][part][:, half * SEQ:(half + 1) * SEQ],
                                       xT_hi, xT_lo)
                        i.then_inc(half_done, 1)

                def ffn_out(slot, b, t, first, last):
                    for h in range(2):
                        i = moving(slot, 2, D, slice(h * 512, (h + 1) * 512), acc[2 * t + h], hT_hi, hT_lo,
                                   2 * b, t, first, last)
                    i.then_inc(half_done, 1)

                def ffn_step(fi, b):
                    at = layer * CHUNKS + fi * 3 + (C_FF + 3 + RING)
                    pe.wait_ge(lo_split, at)
                    ffn_in((C_FF + 2) % RING, 1 - b, 0)
                    pe.wait_ge(lo_split, at + 1)
                    ffn_in(C_FF % RING, 1 - b, 1)
                    pe.wait_ge(lo_split, at + 2)
                    pe.wait_ge(h_lo_done, layer * FB + fi + 1)

                for c, half in ORDER[:2 * C_FF]:
                    if (c, half) == (C_KV, 0):
                        pe.wait_ge(xT_lo_done, layer * 8 + 2)
                    if (c, half) == (C_KV, 1):
                        x_transposes(layer * 4 + 1, 1)
                        pe.wait_ge(xT_lo_done, layer * 8 + 4)
                    if (c, half) == (C_BB, 0):
                        pe.wait_ge(ot_lo_done, layer * VALUES + B_ITEMS // 2)
                    if (c, half) == (C_WO, 0):
                        pe.wait_ge(p_landed, layer * 16 + 16)
                        for kt in range(2):
                            for t in range(TILES):
                                i = nc.tensor.transpose(bank[7][:, kt * SEQ + t * P:kt * SEQ + (t + 1) * P],
                                                        p_nat[:, t, kt * P:(kt + 1) * P], ident[:, :])
                        i.then_inc(pT_done, 1)
                        pe.wait_ge(u_lo_done, layer * 4 + 2)
                    if (c, half) == (C_WO + 1, 0):
                        pe.wait_ge(u_lo_done, layer * 4 + 4)
                    if (c, half) == (C_PP, 0):
                        pe.wait_ge(pT_lo_done, layer + 1)
                    if (c, half) == (C_PG, 0):
                        pe.wait_ge(*taken(layer, (C_PG - 1, 1)))
                        x_transposes(layer * 4 + 2, 0)
                        pe.wait_ge(xT_lo_done, layer * 8 + 6)
                    if (c, half) == (C_PG, 1):
                        x_transposes(layer * 4 + 3, 1)
                        pe.wait_ge(xT_lo_done, layer * 8 + 8)
                    use_half(c, half).then_inc(half_done, 1)
                    if GAP_CHUNK <= c < C_BA:
                        gap(layer, 2 * (c - GAP_CHUNK) + half)

                weights(layer, C_FF)
                ffn_in(C_FF % RING, 0, 0)
                weights(layer, C_FF + 1)
                ffn_in((C_FF + 1) % RING, 0, 1)
                ffn_step(0, 0)
                pe.wait_ge(pg_used, layer * 4 + 4)
                for t in range(TILES):
                    ffn_out((C_FF + 1) % RING, 0, t, True, False)
                with pe.Fori(0, (FB - 3) // 2) as pair:
                    for b in (1, 0):
                        ffn_step(pair * 2 + (2 - b), b)
                        for t in range(TILES):
                            ffn_out((C_FF + 1) % RING, b, t, False, False)
                ffn_step(FB - 2, 1)
                for t in range(TILES):
                    ffn_out((CHUNKS - 2) % RING, 1, t, False, False)
                    if t == 0:
                        weights(layer, CHUNKS - 1)
                        pe.wait_ge(h_lo_done, layer * FB + FB)
                    ffn_out((CHUNKS - 1) % RING, 0, t, False, True)
                x_transposes(layer * 4 + 4, 0)


_INS = ['x', 'p', 'ln_emb_g', 'ln_emb_b', 'w_in', 'b_gate', 'q_norm_g', 'k_norm_g', 'w_branch_a',
        'w_branch_b', 'w_out', 'ln1_g', 'ln1_b', 'w_ffn_in', 'w_ffn_out', 'ln2_g', 'ln2_b',
        'w_ple_proj', 'w_ple_gate']


def shape_tables():
    import numpy as np
    t = np.arange(SEQ)
    diff = t[None, :] - t[:, None]
    dist = np.empty((SEQ, B_GROUPS, SEQ), np.float32)
    for g, (window, dilation) in enumerate(((128, 1), (512, 4), (2048, 16))):
        reach = window // 2 // dilation * dilation
        seen = (np.abs(diff) <= reach) & (diff % dilation == 0)
        dist[:, g, :] = np.where(seen, -np.abs(diff), -1e32)
    dist = dist.reshape(TILES, P, B_GROUPS, SEQ).transpose(1, 0, 2, 3)
    grid_w, axis = 64, HEAD // 2
    inv = (np.float32(10000.0) ** (-np.arange(0, axis, 2, dtype=np.float32) / np.float32(axis))).astype(np.float32)
    row, col = (t // grid_w).astype(np.float32), (t % grid_w).astype(np.float32)
    tables = []
    for pos in (row, col):
        ang = pos[:, None] * inv[None, :]
        tables.append((np.cos(ang), np.sin(ang)))
    cos = np.concatenate([tables[0][0]] * 2 + [tables[1][0]] * 2, axis=1)
    sin = np.concatenate([-tables[0][1], tables[0][1], -tables[1][1], tables[1][1]], axis=1)
    rope = np.stack([cos, sin], axis=1).astype(np.float32).reshape(TILES, P, 2, HEAD).transpose(1, 0, 2, 3)
    return {"dist_table": np.ascontiguousarray(dist), "rope_table": np.ascontiguousarray(rope),
            "identity_table": np.eye(P, dtype=np.float32)}


def kernel(**inputs):
    import numpy as _np
    import concourse.bacc as _bacc
    from concourse import mybir as _mybir
    from concourse.bass_utils import run_bass_kernel_spmd as _run

    nc = _bacc.Bacc("TRN2", target_bir_lowering=False, num_devices=1)
    arrays, args = {}, []
    for name, a in [(n, inputs[n]) for n in _INS] + list(shape_tables().items()):
        a = _np.ascontiguousarray(a)
        arrays[f"in_{name}"] = a
        args.append(nc.dram_tensor(f"in_{name}", a.shape, _mybir.dt.from_np(a.dtype), kind="ExternalInput").ap())
    args.append(nc.dram_tensor("out_0", (1, SEQ, D), F32, kind="ExternalOutput").ap())
    build(nc, *args)
    r = _run(nc, [arrays], core_ids=[0])
    return r.results[0]["out_0"]
```

```python
import concourse.bass as bass
from concourse import mybir
from contextlib import ExitStack

F32 = mybir.dt.float32
F32R = mybir.dt.float32r
ALU = mybir.AluOpType
ACT = mybir.ActivationFunctionType
AX_X = mybir.AxisListType.X

P = 128
D = 1024
SEQ = 256
TILES = SEQ // P
KT = D // P
DEPTH = 2
HEAD = 64
A_HEADS, A_KV = 16, 4
B_GROUPS, B_PER_GROUP = 3, 4
A_Q, A_KVD, B_D = A_HEADS * HEAD, A_KV * HEAD, B_GROUPS * B_PER_GROUP * HEAD
FFN = -(-8 * D // (3 * 256)) * 256
PLE = 256
ALPHA = (2 * DEPTH) ** 0.25
LN_EPS, RMS_EPS = 1e-5, 1e-6
SCALE = HEAD ** -0.5
QA0, KA0 = 0, A_Q
QB0 = A_Q + 2 * A_KVD
KB0, VB0 = QB0 + B_D, QB0 + 2 * B_D
GATE0 = QB0 + 3 * B_D
N_B_HEADS = B_GROUPS * B_PER_GROUP
SLOPE = [2.0 ** (-8.0 * (n + 1) / N_B_HEADS) for n in range(N_B_HEADS)]

WORDS = 2048
RING = 3
C_KV = 0
C_KB, C_QB = 2, 5
C_VB = 8
C_QA = 11
C_GB, C_BB = 15, 19
C_GA, C_BA = 21, 25
C_WO, C_PP, C_PG = 29, 33, 35
C_FF = 39
FB = FFN // 256
CHUNKS = C_FF + 3 * FB
assert CHUNKS == 72 and CHUNKS % RING == 0 and C_FF % RING == 0 and FB % 2 == 1
AHEAD = 2

PAIRS = (C_KV, C_WO + 2, CHUNKS - 2)
ORDER = []
for _c in range(CHUNKS):
    if _c in PAIRS:
        ORDER += [(_c, 0), (_c + 1, 0), (_c, 1), (_c + 1, 1)]
    elif _c - 1 not in PAIRS:
        ORDER += [(_c, 0), (_c, 1)]
assert len(ORDER) == 2 * CHUNKS

GAP_CHUNK = 8
B_ITEMS = B_PER_GROUP * TILES
A_ITEMS = A_HEADS // 2
ITEMS = B_ITEMS + A_ITEMS
VALUES = B_ITEMS // 2 + A_ITEMS
A_GAP = 2 * B_ITEMS - 1
SOFTMAX_GAPS = 3
ROUNDS = {-2: 0, 14: 1, 17: 2, 19: 3, 21: 4}
N_ROUNDS = len(ROUNDS)
SUMS_GAPS = {10: 1, 15: 2}
ROTATE_GAPS = {11: (1, 0), 12: (1, 1), 16: (2, 0), 17: (2, 1)}
POOL_STEPS, TABLES = 17, 13

USES, TAKEN_BY, COMPLETE_AT = [], {}, {}
for _c, _half in ORDER[:2 * C_FF]:
    _pair = _c in (C_KV, C_VB, C_QA, C_QA + 2)
    _alone = C_BB <= _c < C_GA or C_PP <= _c < C_PG
    _both = (C_KB <= _c < C_VB or _c == C_VB + 2 or C_GB <= _c < C_BB
             or C_GA <= _c < C_WO)
    if _pair or _alone or (_both and _half == 0):
        _use = (_c, _half)
        USES.append(_use)
        TAKEN_BY[_use] = "DVE" if C_KB <= _c < C_VB or C_BB <= _c < C_GA or C_BA <= _c < C_WO else "ACT"
        COMPLETE_AT[_use] = ORDER.index((_c + 1, _half) if _pair else (_c, 1) if _both else _use)
    if 2 * (_c - GAP_CHUNK) + _half in ROUNDS:
        _use = ("round", ROUNDS[2 * (_c - GAP_CHUNK) + _half])
        USES.append(_use)
        TAKEN_BY[_use], COMPLETE_AT[_use] = "DVE", ORDER.index((_c, _half)) + 0.5
TAKES = {e: sorted([u for u in USES if TAKEN_BY[u] == e], key=COMPLETE_AT.get) for e in ("ACT", "DVE")}


def narrow(c):
    return c in (C_BB, C_BB + 1, C_PP, C_PP + 1)


def half_at(layer, c, half):
    return layer * (2 * CHUNKS) + (ORDER.index((c, half)) + 1 + 2 * RING)


def slot_free_at(layer, c):
    before = c - RING
    return half_at(layer, before, 1) if before >= 0 else half_at(layer, before + CHUNKS, 1) - 2 * CHUNKS


def scores_item(g):
    if g < 0 or g >= A_GAP + 2 * A_ITEMS:
        return None
    if g < A_GAP:
        return g // 2 if g % 2 == 0 else None
    return B_ITEMS + (g - A_GAP) // 2 if (g - A_GAP) % 2 == 0 else None


def transpose_item(g):
    return scores_item(g - SOFTMAX_GAPS)


def value_pair(g):
    n = transpose_item(g - 1)
    if n is None or (n < B_ITEMS and n % 2 == 0):
        return None
    return n // 2 if n < B_ITEMS else B_ITEMS // 2 + n - B_ITEMS


def build(nc, x, p, ln_emb_g, ln_emb_b, w_in, b_gate, q_norm_g, k_norm_g, w_branch_a, w_branch_b,
          w_out, ln1_g, ln1_b, w_ffn_in, w_ffn_out, ln2_g, ln2_b, w_ple_proj, w_ple_gate,
          dist_table, rope_table, identity_table, out):
    ctx = ExitStack()
    with ctx:
        def sb(name, shape, dt=F32):
            return ctx.enter_context(nc.sbuf_tensor(name, shape, dt))

        def sem(name):
            return ctx.enter_context(nc.semaphore(name))

        w_raw = sb("w_raw", [P, RING, WORDS])
        w_hi = sb("w_hi", [P, RING, WORDS], F32R)
        w_lo = sb("w_lo", [P, RING, WORDS], F32R)
        x_nat = sb("x_nat", [P, TILES, D])
        res = sb("res", [P, TILES, D])
        xT_hi = sb("xT_hi", [P, KT, SEQ], F32R)
        xT_lo = sb("xT_lo", [P, KT, SEQ], F32R)
        ln_gb = sb("ln_gb", [P, 2, D])
        dist = sb("dist", [P, TILES, B_GROUPS, SEQ])
        rope = sb("rope", [P, TILES, 2, HEAD])
        rope_q = sb("rope_q", [P, TILES, 2, HEAD])
        rope_k = sb("rope_k", [P, TILES, 2, HEAD])
        qk_gain = sb("qk_gain", [P, 2, HEAD])
        bias_raw = sb("bias_raw", [P, 2 * KT])
        bias_half = sb("bias_half", [P, 2 * KT])
        ident = sb("ident", [P, P])
        vB = sb("vB", [P, TILES, B_D])
        vA = sb("vA", [P, TILES, A_KVD])
        q_raw = sb("q_raw", [P, TILES, 512])
        q_sq = sb("q_sq", [P, TILES, 512])
        q_rot = sb("q_rot", [P, 2, TILES, 512])
        stack = sb("stack", [P, 6 * KT * P], F32R)
        o_T = sb("o_T", [P, 2, KT, SEQ], F32R)
        oBT_hi = sb("oBT_hi", [P, 2, SEQ], F32R)
        oBT_lo = sb("oBT_lo", [P, 2, SEQ], F32R)
        soft = sb("soft", [P, 3072])
        pT = sb("pT", [P, 4, SEQ], F32R)
        smax = sb("smax", [P, 4, 4])
        nbias = sb("nbias", [P, 4, 4])
        denom = sb("denom", [P, 4, 4])
        rdenom = sb("rdenom", [P, 4, 4])
        head_ms = sb("head_ms", [P, 3, 16])
        head_ve = sb("head_ve", [P, 3, 16])
        head_rstd = sb("head_rstd", [P, 3, 16])
        bn = sb("bn", [P, TILES, 2, 6])
        mean_var = sb("mean_var", [P, TILES, 2])
        ln_ve = sb("ln_ve", [P, TILES])
        ln_rstd = sb("ln_rstd", [P, TILES])
        minus_half = sb("minus_half", [P, 16])

        def heads(ap):
            return ap.rearrange("p (h s) -> p h s", s=SEQ)

        kB = stack[:, :].rearrange("p (h a s) -> p h a s", a=2, s=SEQ)
        kB_hi, kB_lo = kB[:, :, 0, :], kB[:, :, 1, :]
        qA = heads(stack[:, 0:4096])
        kA_hi, kA_lo = pT, heads(o_T[:, :, :, :].rearrange("p a k s -> p (a k s)")[:, 3072:4096])
        pT_hi, pT_lo = pT[:, 0:2, :], pT[:, 2:4, :]
        oAT_hi, oAT_lo = o_T[:, 0, :, :], o_T[:, 1, :, :]
        qB = heads(o_T[:, :, :, :].rearrange("p a k s -> p (a k s)")[:, 0:3072])
        gateB = heads(res[:, :, :].rearrange("p t d -> p (t d)"))
        gateA = heads(q_rot[:, :, :, :].rearrange("p a t n -> p (a t n)"))
        ple = q_rot[:, :, :, :].rearrange("p a t n -> p (a t n)").rearrange("p (t d) -> p t d", t=TILES)
        p_nat = vB[:, :, 0:PLE]
        act_t = q_raw
        hid = q_sq
        hT_hi, hT_lo = oAT_hi, oAT_lo

        psum = ctx.enter_context(nc.psum_tensor("psum", [P, 8, 512], F32))
        bank = [psum[:, b, :] for b in range(8)]
        acc = bank[3:7]
        ffn_bank = [(bank[0], bank[1]), (bank[2], bank[7])]

        def probs_of(n):
            if n < B_ITEMS:
                return soft[:, (n % 2) * 768:(n % 2 + 1) * 768]
            return ln_gb[:, n % 2, :]

        def probsT_of(n):
            if n < B_ITEMS:
                return soft[:, 1536 + (n % 2) * 768:1536 + (n % 2 + 1) * 768]
            return soft[:, (n % 2) * 1024:(n % 2 + 1) * 1024]

        def b_item(n):
            return 2 * (n // 4) + n % 2, (n // 2) % 2

        def b_head(h, group):
            return h * B_GROUPS + group

        def b_places(group, e):
            return slice(b_head(e, group), b_head(e + 2, group) + 1, 2 * B_GROUPS)

        def a_places(r, e):
            first = max(4 * r - 4, 0)
            return slice(first + e, first + 4, 2)

        def use_bank(use):
            return bank[USES.index(use) % 3]

        def taken(layer, use):
            takes = TAKES[TAKEN_BY[use]]
            return proj_act if TAKEN_BY[use] == "ACT" else proj_dve, layer * len(takes) + (takes.index(use) + 1)

        def ot_place(m):
            if m < B_ITEMS // 2:
                cols = slice((m % 2) * P, (m % 2 + 1) * P)
                return oBT_hi[:, m // 2, cols], oBT_lo[:, m // 2, cols], bank[7][:, m * P:(m + 1) * P]
            j = m - B_ITEMS // 2
            return oAT_hi[:, j, :], oAT_lo[:, j, :], bank[7][:, (j % 2) * SEQ:(j % 2 + 1) * SEQ]

        w_landed = [sem(f"w_landed{s}") for s in range(RING)]
        part_landed = sem("part_landed")
        part_split = sem("part_split")
        hi_split = sem("hi_split")
        lo_split = sem("lo_split")
        half_done = sem("half_done")
        columns_done = sem("columns_done")
        x_landed = [sem(f"x_landed{t}") for t in range(TILES)]
        ident_landed = sem("ident_landed")
        rope_landed = sem("rope_landed")
        dist_landed = sem("dist_landed")
        emb_gain_landed = sem("emb_gain_landed")
        emb_bias_landed = sem("emb_bias_landed")
        gb_landed = sem("gb_landed")
        small_landed = sem("small_landed")
        p_landed = sem("p_landed")
        half_set = sem("half_set")
        head_ve_set = sem("head_ve_set")
        pool_steps = sem("pool_steps")
        dve_chain = sem("dve_chain")
        var_ready = sem("var_ready")
        rstd_ready = sem("rstd_ready")
        x_ready = sem("x_ready")
        xT_done = sem("xT_done")
        xT_hi_done = sem("xT_hi_done")
        xT_lo_done = sem("xT_lo_done")
        pT_done = sem("pT_done")
        pT_hi_done = sem("pT_hi_done")
        pT_lo_done = sem("pT_lo_done")
        proj_act = sem("proj_act")
        proj_dve = sem("proj_dve")
        kqB_hi = sem("kqB_hi")
        sq_ready = sem("sq_ready")
        ms_ready = sem("ms_ready")
        head_rstd_ready = sem("head_rstd_ready")
        rotated = sem("rotated")
        qkT_done = sem("qkT_done")
        qkT_hi = sem("qkT_hi")
        scores_done = sem("scores_done")
        nbias_done = sem("nbias_done")
        exp_done = sem("exp_done")
        rdenom_done = sem("rdenom_done")
        probsB_done = sem("probsB_done")
        probsA_done = sem("probsA_done")
        probsT_done = sem("probsT_done")
        probsT_taken = sem("probsT_taken")
        ot_done = sem("ot_done")
        ot_hi_done = sem("ot_hi_done")
        ot_lo_done = sem("ot_lo_done")
        u_done = sem("u_done")
        u_hi_done = sem("u_hi_done")
        u_lo_done = sem("u_lo_done")
        pg_tanh = sem("pg_tanh")
        pg_used = sem("pg_used")
        ff_tanh = sem("ff_tanh")
        h_done = sem("h_done")
        h_hi_done = sem("h_hi_done")
        h_lo_done = sem("h_lo_done")
        out_stored = sem("out_stored")

        def wait_alone(eng, semaphore, value):
            value = value if isinstance(value, int) else eng.to_reg(value)
            eng.wait_ge(semaphore, 1)
            eng.wait_ge(semaphore, value)

        def row_of(vector, n):
            return vector.rearrange("(a d) -> a d", a=1).broadcast_to((P, n))

        block = ctx.enter_context(nc.Block())

        @block.sync
        def _(sp):
            def rows(w, layer, k0, k, c0, n):
                return w[layer, k0 * P:(k0 + k) * P, bass.ds(c0, n)].rearrange("(k p) n -> p k n", p=P)

            def source(layer, c):
                if c < C_KB:
                    return rows(w_in, layer, 4 * (c - C_KV), 4, KA0, 512)
                if c < C_QB:
                    return rows(w_in, layer, 0, KT, KB0 + 256 * (c - C_KB), 256)
                if c < C_VB:
                    return rows(w_in, layer, 0, KT, QB0 + 256 * (c - C_QB), 256)
                if c < C_VB + 2:
                    return rows(w_in, layer, 4 * (c - C_VB), 4, VB0, 512)
                if c == C_VB + 2:
                    return rows(w_in, layer, 0, KT, VB0 + 512, 256)
                if c < C_GB:
                    return rows(w_in, layer, 4 * ((c - C_QA) % 2), 4, QA0 + 512 * ((c - C_QA) // 2), 512)
                if c < C_BB:
                    return rows(w_in, layer, 0, KT, GATE0 + D + 256 * (c - C_GB), 256)
                if c < C_GA:
                    return rows(w_branch_b, layer, 0, 2, 512 * (c - C_BB), 512)
                if c < C_BA:
                    return rows(w_in, layer, 0, KT, GATE0 + 256 * (c - C_GA), 256)
                if c < C_WO:
                    return rows(w_branch_a, layer, 0, KT, 256 * (c - C_BA), 256)
                if c < C_PP:
                    return rows(w_out, layer, 4 * ((c - C_WO) % 2), 4, 512 * ((c - C_WO) // 2), 512)
                if c < C_PG:
                    return rows(w_ple_proj, layer, 0, 2, 512 * (c - C_PP), 512)
                return rows(w_ple_gate, layer, 4 * ((c - C_PG) % 2), 4, 512 * ((c - C_PG) // 2), 512)

            def load(chunk_index, slot, src):
                k, n = src.shape[1], src.shape[2]
                wait_alone(sp, lo_split, chunk_index + 1)
                sp.dma_start(w_raw[:, slot, 0:k * n].rearrange("p (k n) -> p k n", k=k), src)\
                  .then_inc(w_landed[slot], 16)

            for t in range(TILES):
                sp.dma_start(res[:, t, :], x[0, t * P:(t + 1) * P, :]).then_inc(x_landed[t], 16)
                if t == 0:
                    sp.dma_start(ln_gb[:, 1, :], row_of(ln_emb_b, D)).then_inc(emb_bias_landed, 16)
                if t == 0:
                    for part, landed in ((0, part_landed), (1, w_landed[0])):
                        sp.dma_start(w_raw[:, 0, part * 1024:(part + 1) * 1024].rearrange("p (k n) -> p k n", k=2),
                                     source(0, 0)[:, 2 * part:2 * part + 2, :]).then_inc(landed, 16)
                else:
                    load(t, t, source(0, t))
            with sp.Fori(0, DEPTH) as layer:
                for c in range(AHEAD, C_FF):
                    load(layer * CHUNKS + c, c % RING, source(layer, c))
                load(layer * CHUNKS + C_FF, C_FF % RING, rows(w_ffn_in, layer, 0, KT, 0, 256))
                load(layer * CHUNKS + (C_FF + 1), (C_FF + 1) % RING, rows(w_ffn_in, layer, 0, KT, FFN, 256))
                with sp.Fori(0, FB - 1) as f:
                    at = layer * CHUNKS + f * 3 + (C_FF + 2)
                    load(at, (C_FF + 2) % RING, rows(w_ffn_in, layer, 0, KT, f * 256 + 256, 256))
                    load(at + 1, C_FF % RING, rows(w_ffn_in, layer, 0, KT, f * 256 + (FFN + 256), 256))
                    out_rows = w_ffn_out[layer, :, :].rearrange("(b k p) n -> b p k n", k=2, p=P)
                    load(at + 2, (C_FF + 1) % RING, out_rows[f, :, :, :])
                load(layer * CHUNKS + (CHUNKS - 1), (CHUNKS - 1) % RING,
                     rows(w_ffn_out, layer, 2 * (FB - 1), 2, 0, D))
                following = (layer + 1) % DEPTH
                for c in range(AHEAD):
                    load(layer * CHUNKS + (CHUNKS + c), c, source(following, c))
            for t in range(TILES):
                for half in range(2):
                    cols = slice(half * 512, half * 512 + 512)
                    sp.wait_ge(x_ready, 2 * (DEPTH * 4 + t) + half + 1)
                    sp.dma_start(out[0, t * P:(t + 1) * P, cols], x_nat[:, t, cols]).then_inc(out_stored, 16)
            sp.wait_ge(out_stored, 2 * 16 * TILES)

        @block.gpsimd
        def _(pool):
            nc.gpsimd.memset(minus_half[:, :], -0.5).then_inc(half_set, 1)

            def ln_power(t, n, step, eps=4 * LN_EPS):
                wait_alone(pool, var_ready, n)
                nc.gpsimd.tensor_scalar(ln_ve[:, t:t + 1], mean_var[:, t, 1:2], eps, None, ALU.add)\
                    .then_inc(pool_steps, 1)
                pool.wait_ge(pool_steps, step)
                nc.gpsimd.tensor_tensor(ln_rstd[:, t:t + 1], ln_ve[:, t:t + 1], minus_half[:, 0:1], ALU.pow)\
                    .then_inc(rstd_ready, 1)

            def load_gb(layer, g, b):
                pool.dma_start(ln_gb[:, 0, :], row_of(g[layer, :], D)).then_inc(gb_landed, 16)
                pool.dma_start(ln_gb[:, 1, :], row_of(b[layer, :], D)).then_inc(gb_landed, 16)

            def head_power(layer, s):
                n = 8 if s == 0 else 16
                wait_alone(pool, ms_ready, layer * 3 + (s + 1))
                nc.gpsimd.tensor_scalar(head_ve[:, s, 0:n], head_ms[:, s, 0:n], 1.0 / HEAD if s == 0 else 1.0,
                                        RMS_EPS if s == 0 else RMS_EPS / SCALE ** 2, ALU.mult, ALU.add)\
                    .then_inc(head_ve_set, 1)
                wait_alone(pool, head_ve_set, layer * 3 + (s + 1))
                nc.gpsimd.tensor_tensor(head_rstd[:, s, 0:n], head_ve[:, s, 0:n], minus_half[:, 0:n],
                                        ALU.pow).then_inc(head_rstd_ready, 1)

            pool.wait_ge(half_set, 1)
            for t in range(TILES):
                ln_power(t, t + 1, t + 1, LN_EPS)
            pool.dma_start(rope[:, :, :, :], rope_table).then_inc(rope_landed, 16)
            pool.dma_start(dist[:, :, :, :], dist_table).then_inc(dist_landed, 16)
            with pool.Fori(0, DEPTH) as layer:
                steps = layer * POOL_STEPS + TILES
                pool.dma_start(bias_raw[:, :], b_gate[layer, :].rearrange("(k p) -> p k", p=P),
                               allow_slow_non_contiguous=True).then_inc(small_landed, 16)
                pool.dma_start(qk_gain[:, 0, :], row_of(q_norm_g[layer, :], HEAD)).then_inc(small_landed, 16)
                pool.dma_start(qk_gain[:, 1, :], row_of(k_norm_g[layer, :], HEAD)).then_inc(small_landed, 16)
                pool.wait_ge(rope_landed, 16)
                wait_alone(pool, small_landed, layer * 48 + 48)
                nc.gpsimd.tensor_scalar(bias_half[:, :], bias_raw[:, :], 0.5, None, ALU.mult)\
                    .then_inc(pool_steps, 1)
                for part, table in ((0, rope_q), (1, rope_k)):
                    for t in range(TILES):
                        nc.gpsimd.tensor_tensor(table[:, t, 0, :], rope[:, t, 0, :], qk_gain[:, part, :],
                                                ALU.mult).then_inc(pool_steps, 1)
                        for half in range(2):
                            def halves(ap, h):
                                return ap.rearrange("p (a h j) -> p a h j", a=2, h=2)[:, :, h, :]
                            nc.gpsimd.tensor_tensor(halves(table[:, t, 1, :], half),
                                                    halves(rope[:, t, 1, :], half),
                                                    halves(qk_gain[:, part, :], 1 - half),
                                                    ALU.mult).then_inc(pool_steps, 1)
                wait_alone(pool, pool_steps, steps + TABLES)
                for slab in range(3):
                    head_power(layer, slab)
                wait_alone(pool, ot_done, layer * VALUES + B_ITEMS // 2)
                pool.dma_start(p_nat, p[layer, 0, :, :].rearrange("(t p) d -> p t d", p=P))\
                    .then_inc(p_landed, 16)
                wait_alone(pool, probsT_done, layer * ITEMS + ITEMS)
                load_gb(layer, ln1_g, ln1_b)
                for t in range(TILES):
                    ln_power(t, layer * 4 + (TILES + t + 1), steps + (TABLES + t + 1))
                wait_alone(pool, x_ready, layer * 8 + 8)
                load_gb(layer, ln2_g, ln2_b)
                for t in range(TILES):
                    ln_power(t, layer * 4 + (2 * TILES + t + 1), steps + (TABLES + TILES + t + 1))

        @block.scalar
        def _(act):
            def split_hi(free, landed, slot, words=WORDS):
                act.wait_ge(w_landed[slot], landed)
                act.wait_ge(half_done, free)
                nc.scalar.activation(w_hi[:, slot, 0:words], w_raw[:, slot, 0:words], ACT.Copy)\
                    .then_inc(hi_split, 1)

            def x_transposes(n, t):
                for half in range(2):
                    act.wait_ge(xT_done, 2 * n + half + 1)
                    nc.scalar.activation(xT_hi[:, 4 * half:4 * half + 4, t * P:(t + 1) * P],
                                         acc[2 * t + half].rearrange("p (k s) -> p k s", k=4), ACT.Copy)\
                        .then_inc(xT_hi_done, 1)

            def take(layer, c, half, dst, src, last=True):
                act.wait_ge(half_done, half_at(layer, c, half))
                i = nc.scalar.activation(dst, src, ACT.Copy)
                if last:
                    i.then_inc(proj_act, 1)

            def slab(layer, s):
                c = C_KV + 1 if s == 0 else C_QA - 1 + 2 * s
                if s:
                    act.wait_ge(rotated, layer * 3 + s)
                for t in range(TILES):
                    src = use_bank((c - 1, t))
                    if s == 0:
                        take(layer, c, t, q_raw[:, t, 0:256], src[:, 0:256], last=False)
                        take(layer, c, t, vA[:, t, :], src[:, 256:512])
                    else:
                        take(layer, c, t, q_raw[:, t, :], src)

            def squares(layer, s):
                w = 256 if s == 0 else 512
                c = C_KV + 1 if s == 0 else C_QA - 1 + 2 * s
                act.wait_ge(*taken(layer, (c - 1, 1)))
                nc.scalar.activation(q_sq[:, :, 0:w], q_raw[:, :, 0:w], ACT.Square).then_inc(sq_ready, 1)

            def upper_parts(src, e, dst, own, twice):
                rows = slice(HEAD * e, HEAD * e + HEAD)
                for half in range(2) if twice else (e,):
                    i = nc.scalar.activation(dst[HEAD * half:HEAD * half + HEAD, own, :], src[rows, :, :], ACT.Copy)
                return i

            def mixer_b_hi(layer, c):
                act.wait_ge(half_done, half_at(layer, c, 1))
                for e in range(2):
                    i = upper_parts(heads(use_bank((c, 0))), e, kB_hi if c < C_QB else qB, b_places((c - C_KB) % 3, e),
                                    c < C_QB)
                i.then_inc(kqB_hi, 1)

            def gap(layer, g):
                if g in ROUNDS:
                    r = ROUNDS[g]
                    act.wait_ge(qkT_done, layer * N_ROUNDS + (r + 1))
                    for e in range(2):
                        i = upper_parts(heads(use_bank(("round", r))), e, kA_hi if r == 0 else qA, a_places(r, e), r == 0)
                    i.then_inc(qkT_hi, 1)
                n = transpose_item(g)
                if n is not None:
                    act.wait_ge(probsT_done, layer * ITEMS + (n + 1))
                    if 2 <= n < B_ITEMS:
                        act.wait_ge(ot_done, layer * VALUES + n // 2)
                    elif n > B_ITEMS:
                        act.wait_ge(ot_done, layer * VALUES + (B_ITEMS // 2 + n - B_ITEMS - 1))
                    src = psum[:, 5:7, :].rearrange("p b n -> p (b n)")
                    w = 768 if n < B_ITEMS else 1024
                    nc.scalar.activation(probsT_of(n), src[:, 0:w], ACT.Copy).then_inc(probsT_taken, 1)
                m = value_pair(g)
                if m is not None:
                    act.wait_ge(ot_done, layer * VALUES + (m + 1))
                    hi, _, src = ot_place(m)
                    nc.scalar.activation(hi, src, ACT.Copy).then_inc(ot_hi_done, 1)

            def normalise(layer, n):
                if n is not None and n < B_ITEMS:
                    act.wait_ge(rdenom_done, layer * ITEMS + (n + 1))
                    z = probs_of(n)
                    nc.scalar.activation(z, z, ACT.Copy, scale=rdenom[:, n % 4, 0:1]).then_inc(probsB_done, 1)

            def exponentials(layer, g):
                n = scores_item(g)
                if n is not None:
                    act.wait_ge(nbias_done, layer * ITEMS + (n + 1))
                    z = probs_of(n)
                    if n < B_ITEMS:
                        e = nc.scalar.activation(z, z, ACT.Exp, bias=nbias[:, n % 4, 0:1], scale=SCALE,
                                                 accum_out=denom[:, n % 4, 0:1])
                    else:
                        for i in range(4):
                            head, t = 2 * (n - B_ITEMS) + i // 2, i % 2
                            at = t * 8 + head % 8
                            e = nc.scalar.activation(z[:, i * SEQ:(i + 1) * SEQ],
                                                     bank[3 + i // 2][:, t * SEQ:(t + 1) * SEQ], ACT.Exp,
                                                     bias=nbias[:, n % 4, i:i + 1],
                                                     scale=head_rstd[:, 1 + head // 8, at:at + 1],
                                                     accum_out=denom[:, n % 4, i:i + 1])
                    e.then_inc(exp_done, 1)

            act.dma_start(ln_gb[:, 0, :], row_of(ln_emb_g, D)).then_inc(emb_gain_landed, 16)
            act.dma_start(ident[:, :], identity_table).then_inc(ident_landed, 16)
            act.wait_ge(part_landed, 16)
            nc.scalar.activation(w_hi[:, 0, 0:1024], w_raw[:, 0, 0:1024], ACT.Copy).then_inc(part_split, 1)
            act.wait_ge(w_landed[0], 16)
            nc.scalar.activation(w_hi[:, 0, 1024:WORDS], w_raw[:, 0, 1024:WORDS], ACT.Copy).then_inc(hi_split, 1)
            with act.Fori(0, DEPTH) as layer:
                def ahead(c):
                    split_hi(slot_free_at(layer, c + AHEAD), layer * (16 * CHUNKS // RING)
                             + 16 * ((c + AHEAD) // RING + 1), (c + AHEAD) % RING,
                             WORDS // 2 if narrow(c + AHEAD) else WORDS)

                x_transposes(layer * 4, 0)
                ahead(1 - AHEAD)
                x_transposes(layer * 4 + 1, 1)

                def ple_tanh(h, t):
                    n = 2 * h + t
                    act.wait_ge(half_done, half_at(layer, C_PG + 2 * h + 1, t))
                    if n >= 2:
                        act.wait_ge(pg_used, layer * 4 + (n - 1))
                    nc.scalar.activation(act_t[:, n % 2, :], acc[2 * t + h], ACT.Tanh, scale=0.5)\
                        .then_inc(pg_tanh, 1)

                for c in range(C_FF):
                    if not C_VB <= c <= C_BA:
                        ahead(c)
                    for half in range(2):
                        g = 2 * (c - GAP_CHUNK) + half
                        in_gaps = C_VB - 1 <= c < C_BA
                        new_slab = {C_KV + 1: 0, C_QA + 1: 1, C_QA + 3: 2}.get(c) if half == 1 else None
                        if half == 1 and C_KB <= c < C_VB:
                            mixer_b_hi(layer, c)
                        if 0 <= g - 1 < A_GAP:
                            normalise(layer, scores_item(g - 1))
                        if c == C_VB + 1:
                            take(layer, c, half, vB[:, half, 0:512], use_bank((C_VB, half)))
                        if c == C_VB + 2 and half == 1:
                            take(layer, c, 1, vB[:, :, 512:768],
                                 use_bank((c, 0)).rearrange("p (t n) -> p t n", t=TILES))
                        if new_slab is not None:
                            slab(layer, new_slab)
                        urgent = in_gaps and (half == 0 or value_pair(g + 1) is not None) and g < A_GAP
                        if urgent:
                            gap(layer, g)
                        if half == 1 and C_VB <= c + 1 <= C_BA:
                            ahead(c + 1)
                        if in_gaps and not urgent:
                            gap(layer, g)
                        if new_slab is not None:
                            squares(layer, new_slab)
                        if half == 1 and (C_GB <= c < C_BB or C_GA <= c < C_BA):
                            q = c - (C_GB if c < C_BB else C_GA)
                            dst, b0 = (gateB, KT) if c < C_BB else (gateA, 0)
                            act.wait_ge(half_done, half_at(layer, c, 1))
                            src = heads(use_bank((c, 0)))
                            for b in range(2):
                                i = nc.scalar.activation(dst[:, 2 * q + b, :], src[:, b, :],
                                                         ACT.Tanh, scale=0.5,
                                                         bias=bias_half[:, b0 + 2 * q + b:b0 + 2 * q + b + 1])
                            i.then_inc(proj_act, 1)
                        if in_gaps:
                            exponentials(layer, g)
                    if C_BA <= c < C_WO:
                        q = c - C_BA
                        act.wait_ge(u_done, layer * 4 + (q + 1))
                        nc.scalar.activation(xT_hi[:, 2 * q:2 * q + 2, :], gateA[:, 2 * q:2 * q + 2, :],
                                             ACT.Copy).then_inc(u_hi_done, 1)
                    if c == C_WO:
                        act.wait_ge(pT_done, layer + 1)
                        nc.scalar.activation(pT_hi[:, :, :], heads(bank[7]), ACT.Copy).then_inc(pT_hi_done, 1)
                    if C_PP <= c < C_PG:
                        for t in range(TILES):
                            take(layer, c, t, ple[:, t, (c - C_PP) * 512:(c - C_PP + 1) * 512], use_bank((c, t)))
                    if c == C_PP:
                        x_transposes(layer * 4 + 2, 0)
                    if c == C_PP + 1:
                        x_transposes(layer * 4 + 3, 1)
                    if c == C_PG + 1:
                        for t in range(TILES):
                            ple_tanh(0, t)
                    if c == C_PG + 3:
                        for t in range(TILES):
                            ple_tanh(1, t)

                def ffn_tanh(gate_chunk, b):
                    act.wait_ge(half_done, layer * (2 * CHUNKS) + gate_chunk * 2 + (2 + 2 * RING))
                    nc.scalar.activation(act_t[:, b, :], ffn_bank[b][0], ACT.Tanh, scale=0.5)\
                        .then_inc(ff_tanh, 1)

                def hidden_hi(fi, b):
                    act.wait_ge(h_done, layer * FB + fi + 1)
                    nc.scalar.activation(hT_hi[:, 2 * b:2 * b + 2, :], heads(hid[:, b, :]), ACT.Copy)\
                        .then_inc(h_hi_done, 1)

                def ahead_ffn(fi, j, slot):
                    split_hi(layer * (2 * CHUNKS) + fi * 6 + (2 * (C_FF + 2 + j) + 2 * RING),
                             layer * (16 * CHUNKS // RING) + fi * 16 + 16 * ((C_FF + 4 + j) // RING + 1), slot)

                ahead(C_FF)
                ahead(C_FF + 1)
                act.wait_ge(pg_used, layer * 4 + 4)
                ffn_tanh(C_FF, 0)
                hidden_hi(0, 0)
                with act.Fori(0, (FB - 1) // 2) as pair:
                    for b in range(2):
                        f = pair * 2 + b
                        ahead_ffn(f, 0, (C_FF + 4) % RING)
                        ahead_ffn(f, 1, (C_FF + 5) % RING)
                        ffn_tanh(f * 3 + (C_FF + 2), 1 - b)
                        ahead_ffn(f, 2, (C_FF + 6) % RING)
                        hidden_hi(f + 1, 1 - b)

        @block.vector
        def _(dve):
            DC = 400
            used = [0]
            base = [0]

            def link(ins):
                used[0] += 1
                ins.then_inc(dve_chain, 1)
                dve.wait_ge(dve_chain, base[0] + used[0])

            def split_lo(index, slot, words=WORDS):
                dve.wait_ge(hi_split, index + 1)
                nc.vector.tensor_tensor(w_lo[:, slot, 0:words], w_raw[:, slot, 0:words],
                                        w_hi[:, slot, 0:words].bitcast(F32),
                                        ALU.subtract).then_inc(lo_split, 1)

            def statistics(t, half):
                i = nc.vector.bn_stats(bn[:, t, half, :], res[:, t, half * 512:half * 512 + 512])
                if half == 1:
                    used[0] += 1
                    i.then_inc(dve_chain, 1)

            def center(t, n):
                wait_alone(dve, dve_chain, base[0] + used[0])
                nc.vector.bn_aggr(mean_var[:, t, :], bn[:, t, :, :]).then_inc(var_ready, 1)
                dve.wait_ge(var_ready, n + 1)
                used[0] += 1
                nc.vector.scalar_tensor_tensor(x_nat[:, t, :], res[:, t, :], mean_var[:, t, 0:1],
                                               ln_gb[:, 0, :], ALU.subtract, ALU.mult).then_inc(dve_chain, 1)

            def scale(t, n):
                wait_alone(dve, dve_chain, base[0] + used[0])
                dve.wait_ge(rstd_ready, n + 1)
                for half in range(2):
                    cols = slice(half * 512, half * 512 + 512)
                    nc.vector.scalar_tensor_tensor(x_nat[:, t, cols], x_nat[:, t, cols], ln_rstd[:, t:t + 1],
                                                   ln_gb[:, 1, cols], ALU.mult, ALU.add).then_inc(x_ready, 1)

            def x_transposes(n, t, halves=(0, 1)):
                for half in halves:
                    dve.wait_ge(xT_hi_done, 2 * n + half + 1)
                    at = (slice(None), slice(4 * half, 4 * half + 4), slice(t * P, (t + 1) * P))
                    nc.vector.tensor_tensor(xT_lo[at], acc[2 * t + half].rearrange("p (k s) -> p k s", k=4),
                                            xT_hi[at].bitcast(F32), ALU.subtract).then_inc(xT_lo_done, 1)

            def lower_parts(src, e, hi, lo, own, twice):
                rows = slice(HEAD * e, HEAD * e + HEAD)
                for half in range(2) if twice else (1 - e,):
                    i = nc.vector.tensor_tensor(lo[HEAD * half:HEAD * half + HEAD, own, :], src[rows, :, :],
                                                hi[rows, own, :].bitcast(F32), ALU.subtract)
                return i

            def mixer_b_lo(layer, c):
                dve.wait_ge(kqB_hi, layer * 6 + (c - C_KB + 1))
                for e in range(2):
                    i = lower_parts(heads(use_bank((c, 0))), e, *((kB_hi, kB_lo) if c < C_QB else (qB, qB)),
                                    b_places((c - C_KB) % 3, e), c < C_QB)
                i.then_inc(proj_dve, 1)

            def slab_views(s):
                w = 256 if s == 0 else 512
                return w // HEAD, [a[:, :, 0:w].rearrange("p t (h d) -> p t h d", d=HEAD) for a in (q_raw, q_sq)]

            def sums(layer, s):
                nh, (_, sq) = slab_views(s)
                dve.wait_ge(sq_ready, layer * 3 + (s + 1))
                nc.vector.tensor_reduce(head_ms[:, s, 0:2 * nh].rearrange("p (t h) -> p t h", t=TILES), sq,
                                        AX_X, ALU.add).then_inc(ms_ready, 1)

            def rotate(layer, s, t):
                nh, (raw, sq) = slab_views(s)
                table = rope_k if s == 0 else rope_q
                if t == 0:
                    dve.wait_ge(ms_ready, layer * 3 + (s + 1))
                if s == 0 and t == 0:
                    dve.wait_ge(pool_steps, layer * POOL_STEPS + (TABLES + TILES))
                    dve.wait_ge(head_rstd_ready, layer * 3 + 1)
                    rs = head_rstd[:, 0, 0:2 * nh].rearrange("p (t h) -> p t h", t=TILES).unsqueeze(3)\
                        .broadcast_to((P, TILES, nh, HEAD))
                    link(nc.vector.tensor_tensor(raw, raw, rs, ALU.mult))

                def part(ap, h):
                    return ap.rearrange("p h (a b j) -> p h a b j", a=2, b=2)[:, :, :, h, :]
                for half in range(2):
                    sine = table[:, t, 1, :].rearrange("p (a b j) -> p a b j", a=2, b=2)[:, :, half, :]\
                        .unsqueeze(1).broadcast_to((P, nh, 2, 16))
                    i = nc.vector.tensor_tensor(part(sq[:, t, :, :], half), part(raw[:, t, :, :], 1 - half),
                                                sine, ALU.mult)
                link(i)
                cosine = table[:, t, 0, :].unsqueeze(1).broadcast_to((P, nh, HEAD))
                link(nc.vector.tensor_tensor(raw[:, t, :, :], raw[:, t, :, :], cosine, ALU.mult))
                if s == 2 and t == 0:
                    dve.wait_ge(qkT_done, layer * N_ROUNDS + 1)
                w = nh * HEAD
                i = nc.vector.tensor_tensor(q_rot[:, s % 2, t, 0:w], q_raw[:, t, 0:w], q_sq[:, t, 0:w], ALU.add)
                if t == 1:
                    i.then_inc(rotated, 1)

            def maxima(layer, n):
                dve.wait_ge(scores_done, layer * ITEMS + (n + 1))
                if n < B_ITEMS:
                    h, t = b_item(n)
                    if n == 0:
                        dve.wait_ge(dist_landed, 16)
                    if n >= 2:
                        dve.wait_ge(probsT_done, layer * ITEMS + (n - 1))
                    z = probs_of(n)
                    for gr in range(B_GROUPS):
                        i = nc.vector.scalar_tensor_tensor(
                            z[:, gr * SEQ:(gr + 1) * SEQ], dist[:, t, gr, :],
                            SLOPE[gr * B_PER_GROUP + h] / SCALE,
                            bank[3 + gr // 2][:, (gr % 2) * SEQ:(gr % 2 + 1) * SEQ], ALU.mult, ALU.add)
                    link(i)
                    link(nc.vector.reduce_max(smax[:, n % 4, 0:1], z, AX_X))
                    nc.vector.tensor_scalar(nbias[:, n % 4, 0:1], smax[:, n % 4, 0:1], -SCALE, None,
                                            ALU.mult).then_inc(nbias_done, 1)
                else:
                    j = n - B_ITEMS
                    if j >= 2:
                        dve.wait_ge(probsT_done, layer * ITEMS + (n - 1))
                    if j % 4 == 0:
                        dve.wait_ge(head_rstd_ready, layer * 3 + (2 + j // 4))
                    link(nc.vector.reduce_max(smax[:, n % 4, :], psum[:, 3:5, :].rearrange("p b n -> p (b n)")
                                              .rearrange("p (i s) -> p i s", s=SEQ), AX_X))
                    at = (2 * j) % 8
                    scale = head_rstd[:, 1 + j // 4, :].rearrange("p (t h) -> p h t", t=TILES)[:, at:at + 2, :]
                    pairs = [a[:, n % 4, :].rearrange("p (h t) -> p h t", h=2) for a in (nbias, smax)]
                    nc.vector.scalar_tensor_tensor(pairs[0], pairs[1], -1.0, scale, ALU.mult, ALU.mult)\
                        .then_inc(nbias_done, 1)

            def reciprocals(layer, n):
                if n is not None:
                    k = 1 if n < B_ITEMS else 4
                    dve.wait_ge(exp_done, layer * ITEMS + (n + 1))
                    nc.vector.reciprocal(rdenom[:, n % 4, 0:k], denom[:, n % 4, 0:k]).then_inc(rdenom_done, 1)
                    if n >= B_ITEMS:
                        dve.wait_ge(rdenom_done, layer * ITEMS + (n + 1))
                        for i in range(4):
                            z = probs_of(n)[:, i * SEQ:(i + 1) * SEQ]
                            last = nc.vector.tensor_scalar(z, z, rdenom[:, n % 4, i:i + 1], None, ALU.mult)
                        last.then_inc(probsA_done, 1)

            def gap(layer, g):
                n = scores_item(g)
                if n is not None:
                    maxima(layer, n)
                if g > A_GAP:
                    reciprocals(layer, scores_item(g - 1))
                if g in ROUNDS:
                    r = ROUNDS[g]
                    dve.wait_ge(qkT_hi, layer * N_ROUNDS + (r + 1))
                    for e in range(2):
                        i = lower_parts(heads(use_bank(("round", r))), e,
                                        *((kA_hi, kA_lo) if r == 0 else (qA, qA)), a_places(r, e), r == 0)
                    i.then_inc(proj_dve, 1)
                m = value_pair(g)
                if m is not None:
                    hi, lo, src = ot_place(m)
                    dve.wait_ge(ot_hi_done, layer * VALUES + (m + 1))
                    nc.vector.tensor_tensor(lo, src, hi.bitcast(F32), ALU.subtract).then_inc(ot_lo_done, 1)
                if g in SUMS_GAPS:
                    sums(layer, SUMS_GAPS[g])
                if g in ROTATE_GAPS:
                    rotate(layer, *ROTATE_GAPS[g])
                if 0 <= g < A_GAP:
                    reciprocals(layer, scores_item(g))

            dve.sem_inc(lo_split, RING)
            for t in range(TILES):
                dve.wait_ge(x_landed[t], 16)
                for half in range(2):
                    statistics(t, half)
                if t == 0:
                    dve.wait_ge(emb_gain_landed, 16)
                    center(0, 0)
                    dve.wait_ge(emb_bias_landed, 16)
                    scale(0, 0)
                    for part, ready in ((0, part_split), (1, hi_split)):
                        words = slice(part * 1024, (part + 1) * 1024)
                        dve.wait_ge(ready, 1)
                        i = nc.vector.tensor_tensor(w_lo[:, 0, words], w_raw[:, 0, words],
                                                    w_hi[:, 0, words].bitcast(F32), ALU.subtract)
                    i.then_inc(lo_split, 1)
            start = used[0]
            with dve.Fori(0, DEPTH) as layer:
                used[0] = 0
                base[0] = layer * DC + start

                def ahead(c):
                    split_lo(layer * CHUNKS + (c + AHEAD), (c + AHEAD) % RING,
                             WORDS // 2 if narrow(c + AHEAD) else WORDS)

                x_transposes(layer * 4, 0)
                ahead(1 - AHEAD)
                center(1, layer * 4 + 1)
                scale(1, layer * 4 + 1)
                x_transposes(layer * 4 + 1, 1)

                def residual(h, t):
                    cols = slice(h * 512, (h + 1) * 512)
                    dve.wait_ge(half_done, half_at(layer, C_WO + 2 * h + 1, t))
                    link(nc.vector.scalar_tensor_tensor(res[:, t, cols], x_nat[:, t, cols], 2 * ALPHA,
                                                        acc[2 * t + h], ALU.mult, ALU.add))
                    statistics(t, h)

                def ple_add(h, t):
                    n = 2 * h + t
                    cols = slice(h * 512, (h + 1) * 512)
                    dve.wait_ge(pg_tanh, layer * 4 + (n + 1))
                    if n == 0:
                        dve.wait_ge(*taken(layer, (C_PG - 1, 1)))
                    if n < 2:
                        dve.wait_ge(x_ready, 2 * (layer * 4 + (TILES + t + 1)))
                    nc.vector.scalar_tensor_tensor(ple[:, t, cols], act_t[:, n % 2, :], 1.0,
                                                   ple[:, t, cols], ALU.add, ALU.mult).then_inc(pg_used, 1)
                    dve.wait_ge(pg_used, layer * 4 + (n + 1))
                    link(nc.vector.scalar_tensor_tensor(res[:, t, cols], x_nat[:, t, cols], 2 * ALPHA,
                                                        ple[:, t, cols], ALU.mult, ALU.add))

                for c in range(C_FF):
                    if c == C_WO + 3:
                        residual(1, 0)
                        dve.wait_ge(gb_landed, layer * 64 + 32)
                        center(0, layer * 4 + TILES)
                        scale(0, layer * 4 + TILES)
                    if c == C_PP + 1:
                        x_transposes(layer * 4 + 3, 1)
                    late = C_VB - 1 <= c < GAP_CHUNK + B_ITEMS
                    if not late:
                        ahead(c)
                    if c == C_PP:
                        x_transposes(layer * 4 + 2, 0)
                        scale(1, layer * 4 + (TILES + 1))
                    if C_KB <= c < C_VB - 1:
                        mixer_b_lo(layer, c)
                    if c == C_KB:
                        sums(layer, 0)
                    if c == C_QB:
                        for t in range(TILES):
                            rotate(layer, 0, t)
                    for half in range(2):
                        if C_VB - 1 <= c < C_BA:
                            gap(layer, 2 * (c - GAP_CHUNK) + half)
                        if half == 0 and c == C_VB - 1:
                            mixer_b_lo(layer, c)
                        if half == 0 and late:
                            ahead(c)
                    for half in range(2):
                        if C_BB <= c < C_GA:
                            q = 2 * (c - C_BB) + half
                            if q == 0:
                                dve.wait_ge(*taken(layer, (C_BB - 1, 0)))
                            dve.wait_ge(half_done, half_at(layer, c, half))
                            nc.vector.scalar_tensor_tensor(gateB[:, 2 * q:2 * q + 2, :], gateB[:, 2 * q:2 * q + 2, :],
                                                           1.0, heads(use_bank((c, half))), ALU.add, ALU.mult)\
                                .then_inc(proj_dve, 1)
                    if C_BA <= c < C_WO:
                        q = c - C_BA
                        if q == 0:
                            dve.wait_ge(*taken(layer, (C_BA - 1, 0)))
                        ga = gateA[:, 2 * q:2 * q + 2, :]
                        dve.wait_ge(half_done, half_at(layer, c, 1))
                        nc.vector.scalar_tensor_tensor(ga, ga, 1.0, heads(use_bank((c, 0))), ALU.add, ALU.mult)\
                            .then_inc(proj_dve, 1)
                        dve.wait_ge(*taken(layer, (c, 0)))
                        nc.vector.tensor_tensor(ga, ga, gateB[:, 2 * q:2 * q + 2, :], ALU.add).then_inc(u_done, 1)
                        dve.wait_ge(u_hi_done, layer * 4 + (q + 1))
                        nc.vector.tensor_tensor(xT_lo[:, 2 * q:2 * q + 2, :], ga,
                                                xT_hi[:, 2 * q:2 * q + 2, :].bitcast(F32), ALU.subtract)\
                            .then_inc(u_lo_done, 1)
                    if c == C_WO:
                        dve.wait_ge(pT_hi_done, layer + 1)
                        nc.vector.tensor_tensor(pT_lo[:, :, :], heads(bank[7]), pT_hi[:, :, :].bitcast(F32),
                                                ALU.subtract).then_inc(pT_lo_done, 1)
                    if c == C_WO + 1:
                        for t in range(TILES):
                            residual(0, t)
                    if c == C_WO + 3:
                        residual(1, 1)
                        center(1, layer * 4 + (TILES + 1))
                    if c == C_PG + 1:
                        for t in range(TILES):
                            ple_add(0, t)
                    if c == C_PG + 3:
                        for t in range(TILES):
                            ple_add(1, t)

                def hidden(fi, up_chunk, b):
                    dve.wait_ge(ff_tanh, layer * FB + fi + 1)
                    dve.wait_ge(half_done, layer * (2 * CHUNKS) + up_chunk * 2 + (2 + 2 * RING))
                    link(nc.vector.scalar_tensor_tensor(hid[:, b, :], act_t[:, b, :], 1.0, ffn_bank[b][0],
                                                        ALU.add, ALU.mult))
                    nc.vector.tensor_tensor(hid[:, b, :], hid[:, b, :], ffn_bank[b][1], ALU.mult)\
                        .then_inc(h_done, 1)

                def hidden_lo(fi, b):
                    dve.wait_ge(h_hi_done, layer * FB + fi + 1)
                    nc.vector.tensor_tensor(hT_lo[:, 2 * b:2 * b + 2, :], heads(hid[:, b, :]),
                                            hT_hi[:, 2 * b:2 * b + 2, :].bitcast(F32), ALU.subtract)\
                        .then_inc(h_lo_done, 1)

                ahead(C_FF)
                ahead(C_FF + 1)
                hidden(0, C_FF + 1, 0)
                hidden_lo(0, 0)
                before = used[0]
                with dve.Fori(0, (FB - 1) // 2) as pair:
                    base[0] = layer * DC + pair * 2 + start
                    for b in range(2):
                        f = pair * 2 + b
                        at = layer * CHUNKS + f * 3 + (C_FF + 4)
                        split_lo(at, (C_FF + 4) % RING)
                        split_lo(at + 1, (C_FF + 5) % RING)
                        hidden(f + 1, f * 3 + (C_FF + 3), 1 - b)
                        hidden_lo(f + 1, 1 - b)
                        split_lo(at + 2, (C_FF + 6) % RING)
                assert used[0] == before + 2
                used[0] = before + FB - 1
                base[0] = layer * DC + start

                def last_residual(t, h):
                    if h == 0:
                        dve.wait_ge(columns_done, layer * TILES + t + 1)
                    else:
                        dve.wait_ge(half_done, half_at(layer, CHUNKS - 1, t))
                    cols = slice(h * 512, (h + 1) * 512)
                    link(nc.vector.tensor_tensor(res[:, t, cols], res[:, t, cols], acc[2 * t + h], ALU.add))
                    statistics(t, h)

                n = layer * 4 + 2 * TILES
                for h in range(2):
                    last_residual(0, h)
                dve.wait_ge(gb_landed, layer * 64 + 64)
                center(0, layer * 4 + 2 * TILES)
                scale(0, layer * 4 + 2 * TILES)
                for h in range(2):
                    last_residual(1, h)
                assert used[0] < DC
                dve.sem_inc(dve_chain, DC - used[0])
            used[0], base[0] = 0, DEPTH * DC + start
            center(1, DEPTH * 4 + 1)
            scale(1, DEPTH * 4 + 1)

        @block.tensor
        def _(pe):
            def product(dst, l_hi, l_lo, r_hi, r_lo, start, stop):
                nc.tensor.matmul(dst, l_hi, r_hi, start=start, stop=False)
                nc.tensor.matmul(dst, l_hi, r_lo, start=False, stop=False)
                return nc.tensor.matmul(dst, l_lo, r_hi, start=False, stop=stop)

            def weights(layer, c):
                pe.wait_ge(lo_split, layer * CHUNKS + (c + 1 + RING))

            def chunk(slot, k, n):
                return [w[:, slot, 0:k * n].rearrange("p (k n) -> p k n", k=k) for w in (w_hi, w_lo)]

            def stationary(slot, k, n, block_, dst, r_hi, r_lo, before_last=None):
                hi, lo = chunk(slot, k, n)
                cols = slice(block_ * P, (block_ + 1) * P)
                for kt in range(k):
                    if kt == k - 1 and before_last is not None:
                        pe.wait_ge(*before_last)
                    i = product(dst, hi[:, kt, cols], lo[:, kt, cols], r_hi[:, kt, :], r_lo[:, kt, :],
                                kt == 0, kt == k - 1)
                return i

            def moving(slot, k, n, cols, dst, l_hi, l_lo, k0, t, start, stop, between=None):
                hi, lo = chunk(slot, k, n)
                rows = slice(t * P, (t + 1) * P)
                for kt in range(k):
                    if kt >= k - 2 and between is not None:
                        between(kt - (k - 2))
                    i = product(dst, l_hi[:, k0 + kt, rows], l_lo[:, k0 + kt, rows], hi[:, kt, cols],
                                lo[:, kt, cols], start and kt == 0, stop and kt == k - 1)
                return i

            def bank_free(layer, use):
                at = USES.index(use)
                if at >= 3:
                    pe.wait_ge(*taken(layer, USES[at - 3]))

            def x_transposes(n, t, halves=(0, 1)):
                for half in halves:
                    pe.wait_ge(x_ready, 2 * n + half + 1)
                    for k in range(4):
                        kt = 4 * half + k
                        i = nc.tensor.transpose(acc[2 * t + half][:, k * P:(k + 1) * P],
                                                x_nat[:, t, kt * P:(kt + 1) * P], ident[:, :])
                    i.then_inc(xT_done, 1)

            def qk_round(layer, r):
                bank_free(layer, ("round", r))
                slab = 0 if r == 0 else 1 + (r - 1) // 2
                pe.wait_ge(rotated, layer * 3 + (slab + 1))
                for b in range(2):
                    first = P * b + (0 if r == 0 else 2 * P * ((r - 1) % 2))
                    for t in range(TILES):
                        at = b * SEQ + t * P
                        i = nc.tensor.transpose(use_bank(("round", r))[:, at:at + P],
                                                q_rot[:, slab % 2, t, first:first + P], ident[:, :])
                i.then_inc(qkT_done, 1)

            def scores(layer, n):
                if n == 0:
                    pe.wait_ge(*taken(layer, (C_VB - 1, 0)))
                elif n <= B_ITEMS:
                    pe.wait_ge(nbias_done, layer * ITEMS + n)
                else:
                    pe.wait_ge(exp_done, layer * ITEMS + n)
                if n < B_ITEMS:
                    h, t = b_item(n)
                    for gr in range(B_GROUPS):
                        dst = bank[3 + gr // 2][:, (gr % 2) * SEQ:(gr % 2 + 1) * SEQ]
                        own = b_head(h, gr)
                        nc.tensor.matmul(dst, qB[:, own, t * P:(t + 1) * P], kB_hi[:, own, :], start=True, stop=False)
                        i = nc.tensor.matmul(dst, qB[:, own, t * P:(t + 1) * P], kB_lo[:, own, :],
                                             start=False, stop=True)
                else:
                    j = n - B_ITEMS
                    if j % 2 == 0:
                        pe.wait_ge(*taken(layer, ("round", j // 2 + 1)))
                    for e in range(2):
                        for t in range(TILES):
                            dst = bank[3 + e][:, t * SEQ:(t + 1) * SEQ]
                            q = qA[:, 2 * j + e, t * P:(t + 1) * P]
                            nc.tensor.matmul(dst, q, kA_hi[:, j // 2, :], start=True, stop=False)
                            i = nc.tensor.matmul(dst, q, kA_lo[:, j // 2, :], start=False, stop=True)
                i.then_inc(scores_done, 1)

            def transposes(layer, n):
                if n > 0:
                    pe.wait_ge(probsT_taken, layer * ITEMS + n)
                z = probs_of(n)
                flat = psum[:, 5:7, :].rearrange("p b n -> p (b n)")
                if n < B_ITEMS:
                    pe.wait_ge(probsB_done, layer * B_ITEMS + (n + 1))
                    for at in range(0, 768, P):
                        i = nc.tensor.transpose(flat[:, at:at + P], z[:, at:at + P], ident[:, :])
                else:
                    pe.wait_ge(probsA_done, layer * A_ITEMS + (n - B_ITEMS + 1))
                    for e in range(2):
                        for kt in range(2):
                            for t in range(TILES):
                                at = e * 512 + t * SEQ + kt * P
                                to = e * 512 + kt * SEQ + t * P
                                i = nc.tensor.transpose(flat[:, to:to + P], z[:, at:at + P], ident[:, :])
                i.then_inc(probsT_done, 1)

            def values(layer, m):
                _, _, dst = ot_place(m)
                if m > 0:
                    pe.wait_ge(ot_lo_done, layer * VALUES + m)
                if m < B_ITEMS // 2:
                    n = 2 * m + 1
                    pe.wait_ge(probsT_taken, layer * ITEMS + (n + 1))
                    if m == 0:
                        pe.wait_ge(*taken(layer, (C_VB + 2, 0)))
                    for step in range(6):
                        gr, kt = step // 2, step % 2
                        for e in range(2):
                            own = gr * B_PER_GROUP + b_item(n - 1 + e)[0]
                            i = nc.tensor.matmul(dst[HEAD * e:HEAD * e + HEAD, :],
                                                 vB[:, kt, own * HEAD:(own + 1) * HEAD],
                                                 probsT_of(n - 1 + e)[:, step * P:(step + 1) * P],
                                                 start=step == 0, stop=step == 5)
                else:
                    j = m - B_ITEMS // 2
                    pe.wait_ge(probsT_taken, layer * ITEMS + (B_ITEMS + j + 1))
                    for kt in range(2):
                        for e in range(2):
                            i = nc.tensor.matmul(dst[HEAD * e:HEAD * e + HEAD, :],
                                                 vA[:, kt, (j // 2) * HEAD:(j // 2 + 1) * HEAD],
                                                 probsT_of(B_ITEMS + j)[:, e * 512 + kt * SEQ:e * 512 + (kt + 1) * SEQ],
                                                 start=kt == 0, stop=kt == 1)
                i.then_inc(ot_done, 1)

            def gap(layer, g):
                n = scores_item(g)
                if n is not None:
                    scores(layer, n)
                if g in ROUNDS:
                    qk_round(layer, ROUNDS[g])
                n = transpose_item(g)
                if n is not None:
                    transposes(layer, n)
                m = value_pair(g)
                if m is not None:
                    values(layer, m)

            pe.sem_inc(half_done, 2 * RING)
            pe.wait_ge(ident_landed, 16)
            with pe.Fori(0, DEPTH) as layer:
                x_transposes(layer * 4, 0)

                def use_half(c, half):
                    between = None
                    if (c, half) == (C_KV + 1, 0):
                        between = lambda part: x_transposes(layer * 4 + 1, 1, (part,))
                    if (c, half) == (C_PG, 0):
                        between = lambda part: x_transposes(layer * 4 + 3, 1, (part,))
                    s = c % RING
                    if half == 0:
                        weights(layer, c)
                    opened = (c, half) if (c, half) in USES else (c, 0) if (c, 0) in USES else (c - 1, half)
                    if (c, half) in USES:
                        bank_free(layer, opened)
                    if C_KB <= c < C_VB or C_GB <= c < C_BB or C_GA <= c < C_WO:
                        r = (oAT_hi, oAT_lo) if c >= C_BA else (xT_hi, xT_lo)
                        late = (ot_lo_done, layer * VALUES + VALUES) if (c, half) == (C_BA, 0) else None
                        return stationary(s, KT, 256, half, use_bank(opened)[:, half * SEQ:(half + 1) * SEQ], *r,
                                          before_last=late)
                    if C_BB <= c < C_GA:
                        for b in range(2):
                            i = stationary(s, 2, 512, 2 * half + b, use_bank(opened)[:, b * SEQ:(b + 1) * SEQ],
                                           oBT_hi, oBT_lo)
                        return i
                    if c == C_VB + 2:
                        return moving(s, KT, 256, slice(0, 256), use_bank(opened)[:, half * SEQ:(half + 1) * SEQ],
                                      xT_hi, xT_lo, 0, half, True, True)
                    if c < C_GB:
                        first = c in (C_KV, C_VB, C_QA, C_QA + 2)
                        return moving(s, 4, 512, slice(0, 512), use_bank(opened), xT_hi, xT_lo,
                                      0 if first else 4, half, first, not first, between)
                    if C_PP <= c < C_PG:
                        return moving(s, 2, 512, slice(0, 512), use_bank(opened), pT_hi, pT_lo, 0, half, True, True)
                    k, h = ((c - C_WO) if c < C_PP else (c - C_PG)) % 2, \
                        ((c - C_WO) if c < C_PP else (c - C_PG)) // 2
                    return moving(s, 4, 512, slice(0, 512), acc[2 * half + h], xT_hi, xT_lo, 4 * k, half,
                                  k == 0, k == 1, between)

                def ffn_in(slot, b, part):
                    for half in range(2):
                        i = stationary(slot, KT, 256, half, ffn_bank[b][part][:, half * SEQ:(half + 1) * SEQ],
                                       xT_hi, xT_lo)
                        i.then_inc(half_done, 1)

                def ffn_out(slot, b, t, first, last):
                    for h in range(2):
                        i = moving(slot, 2, D, slice(h * 512, (h + 1) * 512), acc[2 * t + h], hT_hi, hT_lo,
                                   2 * b, t, first, last)
                        if last and h == 0:
                            i.then_inc(columns_done, 1)
                    i.then_inc(half_done, 1)

                def ffn_step(fi, b):
                    at = layer * CHUNKS + fi * 3 + (C_FF + 3 + RING)
                    pe.wait_ge(lo_split, at)
                    ffn_in((C_FF + 2) % RING, 1 - b, 0)
                    pe.wait_ge(lo_split, at + 1)
                    ffn_in(C_FF % RING, 1 - b, 1)
                    pe.wait_ge(lo_split, at + 2)
                    pe.wait_ge(h_lo_done, layer * FB + fi + 1)

                for c, half in ORDER[:2 * C_FF]:
                    if c < C_KB:
                        pe.wait_ge(xT_lo_done, 2 * (layer * 4 + half) + (c - C_KV + 1))
                    if (c, half) == (C_BB, 0):
                        pe.wait_ge(ot_lo_done, layer * VALUES + B_ITEMS // 2)
                    if (c, half) == (C_WO, 0):
                        pe.wait_ge(p_landed, layer * 16 + 16)
                        for kt in range(2):
                            for t in range(TILES):
                                i = nc.tensor.transpose(bank[7][:, kt * SEQ + t * P:kt * SEQ + (t + 1) * P],
                                                        p_nat[:, t, kt * P:(kt + 1) * P], ident[:, :])
                        i.then_inc(pT_done, 1)
                        pe.wait_ge(u_lo_done, layer * 4 + 2)
                    if (c, half) == (C_WO + 1, 0):
                        pe.wait_ge(u_lo_done, layer * 4 + 4)
                    if (c, half) == (C_PP, 0):
                        pe.wait_ge(pT_lo_done, layer + 1)
                    if (c, half) == (C_PP + 1, 0):
                        x_transposes(layer * 4 + 2, 0)
                    if C_PG <= c < C_PG + 2:
                        pe.wait_ge(xT_lo_done, 2 * (layer * 4 + (2 + half)) + (c - C_PG + 1))
                    use_half(c, half).then_inc(half_done, 1)
                    if C_VB - 1 <= c < C_BA:
                        gap(layer, 2 * (c - GAP_CHUNK) + half)

                weights(layer, C_FF)
                ffn_in(C_FF % RING, 0, 0)
                weights(layer, C_FF + 1)
                ffn_in((C_FF + 1) % RING, 0, 1)
                ffn_step(0, 0)
                pe.wait_ge(pg_used, layer * 4 + 4)
                for t in range(TILES):
                    ffn_out((C_FF + 1) % RING, 0, t, True, False)
                with pe.Fori(0, (FB - 3) // 2) as pair:
                    for b in (1, 0):
                        ffn_step(pair * 2 + (2 - b), b)
                        for t in range(TILES):
                            ffn_out((C_FF + 1) % RING, b, t, False, False)
                ffn_step(FB - 2, 1)
                for t in range(TILES):
                    ffn_out((CHUNKS - 2) % RING, 1, t, False, False)
                    if t == 0:
                        weights(layer, CHUNKS - 1)
                        pe.wait_ge(h_lo_done, layer * FB + FB)
                    ffn_out((CHUNKS - 1) % RING, 0, t, False, True)


_INS = ['x', 'p', 'ln_emb_g', 'ln_emb_b', 'w_in', 'b_gate', 'q_norm_g', 'k_norm_g', 'w_branch_a',
        'w_branch_b', 'w_out', 'ln1_g', 'ln1_b', 'w_ffn_in', 'w_ffn_out', 'ln2_g', 'ln2_b',
        'w_ple_proj', 'w_ple_gate']


def shape_tables():
    import numpy as np
    t = np.arange(SEQ)
    diff = t[None, :] - t[:, None]
    dist = np.empty((SEQ, B_GROUPS, SEQ), np.float32)
    for g, (window, dilation) in enumerate(((128, 1), (512, 4), (2048, 16))):
        reach = window // 2 // dilation * dilation
        seen = (np.abs(diff) <= reach) & (diff % dilation == 0)
        dist[:, g, :] = np.where(seen, -np.abs(diff), -1e32)
    dist = dist.reshape(TILES, P, B_GROUPS, SEQ).transpose(1, 0, 2, 3)
    grid_w, axis = 64, HEAD // 2
    inv = (np.float32(10000.0) ** (-np.arange(0, axis, 2, dtype=np.float32) / np.float32(axis))).astype(np.float32)
    row, col = (t // grid_w).astype(np.float32), (t % grid_w).astype(np.float32)
    tables = []
    for pos in (row, col):
        ang = pos[:, None] * inv[None, :]
        tables.append((np.cos(ang), np.sin(ang)))
    cos = np.concatenate([tables[0][0]] * 2 + [tables[1][0]] * 2, axis=1)
    sin = np.concatenate([-tables[0][1], tables[0][1], -tables[1][1], tables[1][1]], axis=1)
    rope = np.stack([cos, sin], axis=1).astype(np.float32).reshape(TILES, P, 2, HEAD).transpose(1, 0, 2, 3)
    return {"dist_table": np.ascontiguousarray(dist), "rope_table": np.ascontiguousarray(rope),
            "identity_table": np.eye(P, dtype=np.float32)}


def kernel(**inputs):
    import numpy as _np
    import concourse.bacc as _bacc
    from concourse import mybir as _mybir
    from concourse.bass_utils import run_bass_kernel_spmd as _run

    nc = _bacc.Bacc("TRN2", target_bir_lowering=False, num_devices=1)
    arrays, args = {}, []
    for name, a in [(n, inputs[n]) for n in _INS] + list(shape_tables().items()):
        a = _np.ascontiguousarray(a)
        arrays[f"in_{name}"] = a
        args.append(nc.dram_tensor(f"in_{name}", a.shape, _mybir.dt.from_np(a.dtype), kind="ExternalInput").ap())
    args.append(nc.dram_tensor("out_0", (1, SEQ, D), F32, kind="ExternalOutput").ap())
    build(nc, *args)
    r = _run(nc, [arrays], core_ids=[0])
    return r.results[0]["out_0"]
```
